# Optimizing a Trainium2 kernel written in Bass

```python
import jax
import jax.numpy as jnp
from jax import lax
import numpy as np

D_MODEL = 1024
BATCH = 1
SEQ = 1024
DEPTH = 1

GRID_W = 64
CTX_LEN = 256
FOUR_WIDTH = D_MODEL // 2
FOUR_GROUPS = 4
FOUR_GROUP_DIM = FOUR_WIDTH // FOUR_GROUPS
RET_WIDTH = D_MODEL // 2
RET_HEAD_DIM = 64
RET_HEADS = RET_WIDTH // RET_HEAD_DIM
RET_CHUNK = 128
D_FF = 4 * D_MODEL
N_MOD = 6
ROPE_BASE = 10000.0
EPS = 1e-6
IN_SPLITS = (FOUR_WIDTH,
             FOUR_WIDTH + RET_WIDTH,
             FOUR_WIDTH + 2 * RET_WIDTH,
             FOUR_WIDTH + 3 * RET_WIDTH,
             FOUR_WIDTH + 4 * RET_WIDTH,
             FOUR_WIDTH + 4 * RET_WIDTH + D_MODEL)
IN_COLS = FOUR_WIDTH + 4 * RET_WIDTH + 2 * D_MODEL
K_OFF = IN_SPLITS[1]
V_OFF = IN_SPLITS[2]

kernel_name = 'hybrid_fourier_retention_dit_block'

def _rms_norm(x, gain):
    xf = x.astype(jnp.float32)
    y = xf * lax.rsqrt(jnp.mean(xf * xf, axis=-1, keepdims=True) + EPS)
    return (y * gain.astype(jnp.float32)).astype(x.dtype)

def _modulate(h, shift, scale):
    return h * (1.0 + scale) + shift

def _to_heads(t):
    b, l, _ = t.shape
    return t.reshape(b, l, RET_HEADS, RET_HEAD_DIM).transpose(0, 2, 1, 3)

def _rope_tables(rows):
    nf = RET_HEAD_DIM // 4
    inv = ROPE_BASE ** (-jnp.arange(nf, dtype=jnp.float32) / nf)
    r, cc = jnp.meshgrid(jnp.arange(rows, dtype=jnp.float32),
                         jnp.arange(GRID_W, dtype=jnp.float32), indexing='ij')
    ang = jnp.concatenate([r.reshape(-1)[:, None] * inv, cc.reshape(-1)[:, None] * inv], axis=-1)
    return jnp.cos(ang), jnp.sin(ang)

def _apply_rope(t, cos, sin):
    half = t.shape[-1] // 2
    cos = cos.astype(t.dtype)
    sin = sin.astype(t.dtype)
    t1, t2 = t[..., :half], t[..., half:]
    return jnp.concatenate([t1 * cos - t2 * sin, t1 * sin + t2 * cos], axis=-1)

def _retention_chunkwise(q, k, v, log_gamma, s0):
    b, h, l, dk = q.shape
    dv = v.shape[-1]
    n = l // RET_CHUNK
    dt = q.dtype
    pos = jnp.arange(RET_CHUNK, dtype=jnp.float32)
    diff = pos[:, None] - pos[None, :]
    lg = log_gamma[:, None, None]
    intra_decay = jnp.where(diff >= 0, jnp.exp(lg * jnp.maximum(diff, 0.0)), 0.0).astype(dt)
    q_decay = jnp.exp(log_gamma[:, None] * (pos + 1.0)).astype(dt)
    k_decay = jnp.exp(log_gamma[:, None] * (RET_CHUNK - 1.0 - pos)).astype(dt)
    chunk_decay = jnp.exp(log_gamma * RET_CHUNK).astype(dt)
    qc = q.reshape(b, h, n, RET_CHUNK, dk)
    kc = k.reshape(b, h, n, RET_CHUNK, dk)
    vc = v.reshape(b, h, n, RET_CHUNK, dv)
    scores = jnp.einsum('bhnid,bhnjd->bhnij', qc, kc) * intra_decay[None, :, None]
    o_intra = jnp.einsum('bhnij,bhnjv->bhniv', scores, vc)
    kv = jnp.einsum('bhncd,bhncv->nbhdv', kc * k_decay[None, :, None, :, None], vc)

    def step(state, kv_n):
        return chunk_decay[None, :, None, None] * state + kv_n, state

    s_final, s_prev = lax.scan(step, s0.astype(dt), kv)
    o_inter = jnp.einsum('bhncd,nbhdv->bhncv', qc * q_decay[None, :, None, :, None], s_prev)
    return (o_intra + o_inter).reshape(b, h, l, dv), s_final

def _retention_final_state(k, v, log_gamma):
    l = k.shape[2]
    w = jnp.exp(log_gamma[:, None] * (l - 1.0 - jnp.arange(l, dtype=jnp.float32))).astype(k.dtype)
    return jnp.einsum('bhld,bhlv->bhdv', k * w[None, :, :, None], v)

def _bidir_retention(q, k, v, log_gamma, s_f, s_b):
    o_f, sf_out = _retention_chunkwise(q, k, v, log_gamma[0], s_f)
    o_b, sb_out = _retention_chunkwise(jnp.flip(q, 2), jnp.flip(k, 2), jnp.flip(v, 2), log_gamma[1], s_b)
    return o_f + jnp.flip(o_b, 2), sf_out, sb_out

def _fourier_mix(u):
    b, l, _ = u.shape
    ug = u.astype(jnp.float32).reshape(b, l, FOUR_GROUPS, FOUR_GROUP_DIM)
    f = jnp.fft.fft2(ug, axes=(1, 3), norm='ortho').real
    return f.reshape(b, l, FOUR_WIDTH).astype(u.dtype)

def _merge(u, o, g, gate_a, gate_b, four_w_out, gn_gain, ret_w_out, w_out):
    y_four = _fourier_mix(u) @ four_w_out
    b, h, l, dv = o.shape
    of = o.astype(jnp.float32)
    of = of * lax.rsqrt(jnp.mean(of * of, axis=-1, keepdims=True) + EPS)
    o_n = of.transpose(0, 2, 1, 3).reshape(b, l, h * dv).astype(u.dtype) * gn_gain
    y_ret = (jax.nn.silu(g) * o_n) @ ret_w_out
    y = jax.nn.sigmoid(gate_a) * y_four + jax.nn.sigmoid(gate_b) * y_ret
    return y @ w_out

def _token_mixer(h_x, h_c, w_in, four_w_out, log_gamma, gn_gain, ret_w_out, w_out, with_ctx_out):
    scale = RET_HEAD_DIM ** -0.5
    u, q, k, v, g, ga, gb = jnp.split(h_x @ w_in, list(IN_SPLITS), axis=-1)
    rows = h_x.shape[1] // GRID_W
    cos, sin = _rope_tables(rows)
    q = _apply_rope(_to_heads(q), cos, sin)
    k = _apply_rope(_to_heads(k), cos, sin) * scale
    v = _to_heads(v)
    if with_ctx_out:
        uc, qc, kc, vc, gc, gac, gbc = jnp.split(h_c @ w_in, list(IN_SPLITS), axis=-1)
        qc = _to_heads(qc)
        kc = _to_heads(kc) * scale
        vc = _to_heads(vc)
        zero = jnp.zeros((qc.shape[0], RET_HEADS, RET_HEAD_DIM, RET_HEAD_DIM), qc.dtype)
        oc, s_f, s_b = _bidir_retention(qc, kc, vc, log_gamma, zero, zero)
        y_c = _merge(uc, oc, gc, gac, gbc, four_w_out, gn_gain, ret_w_out, w_out)
    else:
        kc = _to_heads(h_c @ w_in[:, K_OFF:K_OFF + RET_WIDTH]) * scale
        vc = _to_heads(h_c @ w_in[:, V_OFF:V_OFF + RET_WIDTH])
        s_f = _retention_final_state(kc, vc, log_gamma[0])
        s_b = _retention_final_state(jnp.flip(kc, 2), jnp.flip(vc, 2), log_gamma[1])
        y_c = None
    o, _, _ = _bidir_retention(q, k, v, log_gamma, s_f, s_b)
    y_x = _merge(u, o, g, ga, gb, four_w_out, gn_gain, ret_w_out, w_out)
    return y_x, y_c

def _sq_relu_mlp(h, w1, w2):
    return jnp.square(jax.nn.relu(h @ w1)) @ w2

def setup_inputs(seed: int = 0) -> dict:
    key = jax.random.key(seed)
    ks = jax.random.split(key, 18)
    f32 = jnp.float32

    def nrm(k, shape, s):
        return jax.random.normal(k, shape, f32) * s

    logit0 = jnp.log(2.0 ** (5.0 + jnp.arange(RET_HEADS, dtype=f32)) - 1.0)
    return {
        'x': nrm(ks[0], (BATCH, SEQ, D_MODEL), 1.0),
        'c': nrm(ks[1], (BATCH, D_MODEL), 1.0),
        'ctx': nrm(ks[2], (BATCH, CTX_LEN, D_MODEL), 1.0),
        'c_ctx': nrm(ks[3], (D_MODEL,), 1.0),
        'w_ada': nrm(ks[4], (DEPTH, D_MODEL, N_MOD * D_MODEL), 0.5 * D_MODEL ** -0.5),
        'b_ada': nrm(ks[5], (DEPTH, N_MOD * D_MODEL), 0.01),
        'norm1_gain': 1.0 + nrm(ks[6], (DEPTH, D_MODEL), 0.02),
        'w_in': nrm(ks[7], (DEPTH, D_MODEL, IN_COLS), D_MODEL ** -0.5),
        'four_w_out': nrm(ks[8], (DEPTH, FOUR_WIDTH, D_MODEL), FOUR_WIDTH ** -0.5),
        'ret_decay_logit': logit0[None, None, :] + nrm(ks[9], (DEPTH, 2, RET_HEADS), 0.1),
        'ret_gn_gain': 1.0 + nrm(ks[10], (DEPTH, RET_WIDTH), 0.02),
        'ret_w_out': nrm(ks[11], (DEPTH, RET_WIDTH, D_MODEL), RET_WIDTH ** -0.5),
        'w_out': nrm(ks[12], (DEPTH, D_MODEL, D_MODEL), D_MODEL ** -0.5),
        'norm2_gain': 1.0 + nrm(ks[13], (DEPTH, D_MODEL), 0.02),
        'w_mlp1': nrm(ks[14], (DEPTH, D_MODEL, D_FF), D_MODEL ** -0.5),
        'w_mlp2': nrm(ks[15], (DEPTH, D_FF, D_MODEL), D_FF ** -0.5),
        'final_gain': 1.0 + nrm(ks[16], (D_MODEL,), 0.02),
    }

def reference(x, c, ctx, c_ctx, w_ada, b_ada, norm1_gain, w_in, four_w_out, ret_decay_logit,
              ret_gn_gain, ret_w_out, w_out, norm2_gain, w_mlp1, w_mlp2, final_gain):
    for l in range(DEPTH):
        with_ctx_out = l < DEPTH - 1
        mod_x = jax.nn.silu(c) @ w_ada[l] + b_ada[l]
        mod_c = jax.nn.silu(c_ctx) @ w_ada[l] + b_ada[l]
        sh1, sc1, g1, sh2, sc2, g2 = jnp.split(mod_x[:, None, :], N_MOD, axis=-1)
        csh1, csc1, cg1, csh2, csc2, cg2 = jnp.split(mod_c, N_MOD, axis=-1)
        log_gamma = jax.nn.log_sigmoid(ret_decay_logit[l].astype(jnp.float32))

        h_x = _modulate(_rms_norm(x, norm1_gain[l]), sh1, sc1)
        h_c = _modulate(_rms_norm(ctx, norm1_gain[l]), csh1, csc1)
        y_x, y_c = _token_mixer(h_x, h_c, w_in[l], four_w_out[l], log_gamma, ret_gn_gain[l],
                                ret_w_out[l], w_out[l], with_ctx_out)
        x = x + g1 * y_x
        h2 = _modulate(_rms_norm(x, norm2_gain[l]), sh2, sc2)
        x = x + g2 * _sq_relu_mlp(h2, w_mlp1[l], w_mlp2[l])

        if with_ctx_out:
            ctx = ctx + cg1 * y_c
            hc2 = _modulate(_rms_norm(ctx, norm2_gain[l]), csh2, csc2)
            ctx = ctx + cg2 * _sq_relu_mlp(hc2, w_mlp1[l], w_mlp2[l])
    return _rms_norm(x, final_gain)


_drawn_inputs = setup_inputs


def setup_inputs(seed=0):
    import zlib

    import numpy as np

    out = dict(_drawn_inputs(seed))
    spreads = {}
    factors = {'b_ada': 3.456,
     'norm1_gain': 8.0,
     'ret_gn_gain': 8.0,
     'norm2_gain': 17.366,
     'final_gain': 8.21}
    for name, (base, spread) in spreads.items():
        noise = np.random.default_rng([zlib.crc32(name.encode()), seed]).standard_normal(out[name].shape)
        drawn = base * np.exp(spread * noise) if base else spread * noise
        out[name] = jnp.asarray(drawn.astype(out[name].dtype))
    for name, factor in factors.items():
        out[name] = (out[name] * factor).astype(out[name].dtype)
    return out
```

```python
from contextlib import ExitStack

import concourse.bass as bass
from concourse import mybir
import numpy as np

F32 = mybir.dt.float32
F32R = mybir.dt.float32r
ALU = mybir.AluOpType
ACT = mybir.ActivationFunctionType
AX = mybir.AxisListType

P = 128
D = 1024
SEQ = 1024
CTX = 256
DFF = 4 * D
KT = D // P
NT = SEQ // P
NC_ = CTX // P
HEADS = 8
HD = 64
PAIRS = HEADS // 2
RW = HEADS * HD
GROUPS = 4
HALF = SEQ // 2
EPS = 1e-6
RING = 6
CW = 1024
FFB = 4
BLOCKS = DFF // P // FFB

STREAM = ([("k", i) for i in range(4)] + [("v", i) for i in range(4)] + [("q", i) for i in range(4)]
          + [("g", i) for i in range(4)] + [("u", i) for i in range(4)] + [("cs", i) for i in range(4)]
          + [(kind, m) for m in range(KT) for kind in ("ga", "gb", "fr")])
STREAM += [("wo", _i) for _i in range(4)] + [("y", _i) for _i in range(7)] + [("wo", _i) for _i in range(4, 8)]
INDEX = {c: i for i, c in enumerate(STREAM)}
RINGED = [c for c in STREAM if c[0] != "y"]
RIDX = {c: i for i, c in enumerate(RINGED)}
RELEASED_EARLY = [c for c in RINGED if c[0] in ("k", "v", "q", "g", "wo") and c[1] % 4 < 3]
MLP0 = len(STREAM)
MLPR = len(RINGED)
W_KINDS = ("k", "v", "q", "g", "u", "ga", "gb", "wo")
WIDX = {c: i for i, c in enumerate(c for c in STREAM if c[0] in W_KINDS)}

TILES = ["c0", "c1"] + list(range(NT))
VTILES = ["c0", "c1"] + list(range(NT - 1, -1, -1))
MAIN = ([("k", t) for t in TILES] + [("v", t) for t in VTILES] + [("q", t) for t in range(NT)]
        + [("g", t) for t in range(NT)] + [("u", g, h) for g in range(GROUPS) for h in range(2)])
MIDX = {c: i for i, c in enumerate(MAIN)}
SIDE = [("x", 0, 0), ("x", 0, 1), ("x", 1, 0), ("x", 1, 1)]
for _s in range(10):
    if _s >= 3:
        SIDE += [("kt", _s - 3)]
    if _s + 2 < 10:
        SIDE += [("x", _s + 2, 0), ("x", _s + 2, 1)]
SIDE += [("kt", 7)] + [("kv", t) for t in range(7, 0, -1)] + [("kv", 0)]
for _j in range(1, 18):
    if _j - 1 < 8:
        SIDE += [("qt", _j - 1)]
    if 10 <= _j <= 17:
        SIDE += [("rt", _j - 10)]
SIDE += [("z", t, h) for t in range(NT) for h in range(2)]
SIDX = {c: i for i, c in enumerate(SIDE)}


def program(nc, ins, out):
    with ExitStack() as ctx:
        def sem(name):
            return ctx.enter_context(nc.semaphore(name))

        arena = ctx.enter_context(nc.sbuf_tensor("arena", [P, 53200], F32))
        base = 16512
        at = {}

        def place(name, off, shape, dt=F32):
            size = int(np.prod(shape[1:])) * 4
            assert base + off + size <= 229344, (name, off, size)
            at[name] = nc.alloc_sbuf_tensor_at(name, shape, dt, offset=base + off)
            return at[name]

        ring_hi = place("ring_hi", 0, [P, RING, CW], F32R)
        ring_lo = place("ring_lo", 24576, [P, RING, CW], F32R)
        raw = place("raw", 49152, [P, 2, CW])
        o_ht = 57344
        ada_in = place("ada_in", o_ht, [P, KT, 2 * D])
        hT_hi = place("hT_hi", o_ht, [P, KT, SEQ], F32R)
        hT_lo = place("hT_lo", o_ht + 32768, [P, KT, SEQ], F32R)
        yT_hi = place("yT_hi", o_ht, [P, KT, SEQ], F32R)
        yT_lo = place("yT_lo", o_ht + 32768, [P, KT, SEQ], F32R)
        h2_hi = place("h2_hi", o_ht, [P, KT, SEQ], F32R)
        h2_lo = place("h2_lo", o_ht + 32768, [P, KT, SEQ], F32R)
        o_kt = o_ht + 65536
        o_qt, o_kv, o_v = o_kt + 16384, o_kt + 32768, o_kt + 49152
        o_m = o_kt + 65536
        x_a = place("x_a", o_kt, [P, 3, D])
        x_b = place("x_b", o_v, [P, 4, D])
        ctx_in = place("ctx_in", o_kv, [P, 2, D])
        mod_rows = place("mod_rows", o_kv + 8192, [2, 2 * D])
        hc_hi = place("hc_hi", o_qt, [P, KT, CTX], F32R)
        hc_lo = place("hc_lo", o_qt + 8192, [P, KT, CTX], F32R)
        kT = place("kT", o_kt, [P, PAIRS, SEQ])
        qT = place("qT", o_qt, [P, PAIRS, SEQ])
        kv = place("kv", o_kv, [P, NT, RW])
        v = place("v", o_v, [P, NT, RW])
        vcat_c = place("vcat_c", o_v, [P, 2, 2 * RW])
        rT_hi = place("rT_hi", o_kt, [P, PAIRS, SEQ], F32R)
        rT_lo = place("rT_lo", o_qt, [P, PAIRS, SEQ], F32R)
        u_e = place("u_e", o_v, [P, GROUPS, HALF])
        u_o = place("u_o", o_v + 8192, [P, GROUPS, HALF])
        fj = place("fj", o_kv, [P, HALF])
        pa_hi = place("pa_hi", o_kv, [P, 4, 256], F32R)
        pa_lo = place("pa_lo", o_kv + 4096, [P, 4, 256], F32R)
        pb_hi = place("pb_hi", o_kv + 8192, [P, 4, 256], F32R)
        pb_lo = place("pb_lo", o_kv + 12288, [P, 4, 256], F32R)
        ab_hi = place("ab_hi", o_v, [P, 4, HALF], F32R)
        ab_lo = place("ab_lo", o_v + 8192, [P, 4, HALF], F32R)
        y = place("y", o_kv, [P, SEQ])
        sig_a = place("sig_a", o_kv + 4096, [P, SEQ])
        sig_b = place("sig_b", o_kv + 8192, [P, SEQ])
        ada_raw = place("ada_raw", o_kv + 12288, [P, D])
        wn_raw = place("wn_raw", o_kv, [GROUPS, D])
        acc = place("acc", o_kt, [P, NT, D])
        g1b = place("g1b", o_kv, [P, D])
        b1b = place("b1b", o_kv + 4096, [P, D])
        b2b = place("b2b", o_kv + 8192, [P, D])
        xh = place("xh", o_kv + 12288, [P, D])
        h2_f = place("h2_f", o_kv + 16384, [P, D])
        xh_b = place("xh_b", o_kv + 28672, [P, D])
        gated = place("gated", o_kv + 20480, [P, 512])
        junk2 = place("junk2", o_kv + 24576, [P, D])
        ff_hi = place("ff_hi", o_kv, [P, FFB, SEQ], F32R)
        ff_lo = place("ff_lo", o_kv + 16384, [P, FFB, SEQ], F32R)
        pos = [o_m]

        def small(name, shape, dt=F32):
            t = place(name, pos[0], shape, dt)
            pos[0] += (int(np.prod(shape[1:])) * 4 + 31) // 32 * 32
            return t

        ident = small("ident", [P, P])
        cc = small("cc", [P, KT, 2])
        silu_c = small("silu_c", [P, KT, 2])
        gain1 = small("gain1", [P, KT])
        gain2 = small("gain2", [P, KT])
        mod = small("mod", [P, 2 * KT, 2])
        a1 = small("a1", [P, KT, 2])
        mod2 = small("mod2", [P, 2, KT])
        bmod2 = small("bmod2", [P, 2, KT])
        a2 = small("a2", [P, KT])
        ss = small("ss", [P, 16])
        ms = small("ms", [P, 16])
        rt = small("rt", [P, 16])
        rstd = small("rstd", [P, 16])
        lgt = small("lgt", [P, 16])
        lw = small("lw", [P, 6, 16])
        lg = small("lg", [P, 16])
        posc = small("posc", [P, 5, 16])
        dec = small("dec", [P, 5, 16])
        dec_s = small("dec_s", [P, PAIRS, 2])
        coef = small("coef", [P, 4])
        hss = small("hss", [P, 8, 4])
        u_c = small("u_c", [P, 2, GROUPS])
        cols = small("cols", [P, 2, 2])
        cols_n = small("cols_n", [GROUPS, 4])
        a5_hi = small("a5_hi", [P, 2, 2], F32R)
        a5_lo = small("a5_lo", [P, 2, 2], F32R)
        n5_hi = small("n5_hi", [GROUPS, 2], F32R)
        n5_lo = small("n5_lo", [GROUPS, 2], F32R)
        pn_hi = small("pn_hi", [P, 4, GROUPS], F32R)
        pn_lo = small("pn_lo", [P, 4, GROUPS], F32R)
        ones = small("ones", [P, 1])
        o_t = pos[0]
        dmask = place("dmask", o_t, [P, HEADS, P])
        rope = place("rope", o_t + 4096, [P, NT, 2, HD // 2])
        h_f = place("h_f", o_t + 6144, [P, D])
        wp_v = place("wp_v", o_t + 6144, [P, 2, 512])
        wp_g = place("wp_g", o_t + 10240, [P, 2, 512])
        aT = place("aT", o_t + 6144, [P, HEADS, P])
        t1 = place("t1", o_t + 10240, [P, 2, RW])
        dist = place("dist", o_t + 10240, [P, 4, P])
        dtmp = place("dtmp", o_t + 12288, [P, 3, P])
        k_c = place("k_c", o_t + 14336, [P, 2, RW])
        junk = place("junk", o_t + 14336, [P, D])
        vcat = place("vcat", o_t + 10240, [P, 2, 2 * RW])
        it = place("it", o_t + 10240, [P, 4, 2, HD])
        st_f = place("st_f", o_t + 12288, [P, 2, PAIRS, HD])
        sq = place("sq", o_t + 14336, [P, RW])
        qb = place("qb", o_t + 16384, [P, RW])
        qa = place("qa", o_t + 18432, [P, RW])
        st_b = place("st_b", o_t + 18432, [P, 2, PAIRS, HD])
        gnb = place("gnb", o_t + 4096, [P, RW])
        sg = place("sg", o_t + 16384, [P, 2, RW])
        mcs = place("mcs", o_t, [P, 2, P])
        u_lo = place("u_lo", o_t + 3072, [P, HALF])
        sgn = place("sgn", o_t + 1024, [P, HALF])
        ft = place("ft", o_t + 5120, [P, HALF])
        an_hi = place("an_hi", o_t + 8192, [GROUPS, HALF], F32R)
        an_lo = place("an_lo", o_t + 10240, [GROUPS, HALF], F32R)
        wn_hi = place("wn_hi", o_t + 12288, [GROUPS, D], F32R)
        wn_lo = place("wn_lo", o_t + 16384, [GROUPS, D], F32R)
        b_sb = place("b_sb", o_t, [P, HALF])
        ada_acc = place("ada_acc", o_t + 2048, [P, D])
        ada_row = place("ada_row", o_t + 6144, [1, 512])
        x_hi = place("x_hi", o_t, [P, 2, CW], F32R)
        x_lo = place("x_lo", o_t + 8192, [P, 2, CW], F32R)
        g2b = place("g2b", o_t + 16384, [P, D])
        fgb = place("fgb", o_t, [P, D])
        o_sb = place("o_sb", o_t + 4096, [P, 2, D])
        junk3 = place("junk3", o_t + 12288, [P, D])

        ps = ctx.enter_context(nc.psum_tensor("ps", [P, 8, 512], F32))

        y_scr = nc.dram_tensor("y_scr", [KT, P, SEQ], F32, kind="Internal").ap()
        wpm_scr = nc.dram_tensor("wpm_scr", [KT, P, 512], F32, kind="Internal").ap()
        mod_scr = nc.dram_tensor("mod_scr", [4, D], F32, kind="Internal").ap()

        raw_in = [sem("raw_in0"), sem("raw_in1")]
        hi_done = sem("hi_done")
        split = sem("split")
        used = sem("used")
        first_in = sem("first_in")
        decay_in = sem("decay_in")
        params_in = sem("params_in")
        ada_landed = [sem(f"ada_landed{i}") for i in range(KT)]
        x_landed = [sem(f"x_landed{i}") for i in range(10)]
        late_in = sem("late_in")
        silu_done = sem("silu_done")
        ada_done = sem("ada_done")
        rows_done = sem("rows_done")
        modT_done = sem("modT_done")
        mod_ready = sem("mod_ready")
        act_step = sem("act_step")
        dve_step = sem("dve_step")
        pool_step = sem("pool_step")
        sumsq = sem("sumsq")
        meansq = sem("meansq")
        root = sem("root")
        xhat = sem("xhat")
        hhi_done = sem("hhi_done")
        h_ready = sem("h_ready")
        main_done = sem("main_done")
        main_free = [sem("main_free0"), sem("main_free1")]
        side_done = sem("side_done")
        side_free = [sem("side_free0"), sem("side_free1")]
        decay_log = sem("decay_log")
        decay_exp = sem("decay_exp")
        decays_ready = sem("decays_ready")
        roped = sem("roped")
        vcat_ready = sem("vcat_ready")
        states_ready = sem("states_ready")
        kvc_done = sem("kvc_done")
        scores_done = sem("scores_done")
        masked = sem("masked")
        intra_done = sem("intra_done")
        inter_done = sem("inter_done")
        combined = sem("combined")
        o_ready = sem("o_ready")
        silu_g = sem("silu_g")
        r_ready = sem("r_ready")
        wp_in = sem("wp_in")
        wpm_stored = sem("wpm_stored")
        ue_ready = sem("ue_ready")
        uc_ready = sem("uc_ready")
        cols_done = sem("cols_done")
        cols_free = sem("cols_free")
        pq_done = sem("pq_done")
        pq_free = sem("pq_free")
        dft_done = sem("dft_done")
        ab_ready = sem("ab_ready")
        wn_in = sem("wn_in")
        wn_ready = sem("wn_ready")
        merge_done = sem("merge_done")
        gates_done = sem("gates_done")
        four_free = sem("four_free")
        col_free = sem("col_free")
        ret_free = sem("ret_free")
        y_ready = sem("y_ready")
        y_stored = sem("y_stored")
        y7_ready = sem("y7_ready")
        ada_raw_in = sem("ada_raw_in")
        ada_acc_done = sem("ada_acc_done")
        ada_red = sem("ada_red")
        ada_row_out = sem("ada_row_out")
        row_stored = sem("row_stored")
        acc_in = [sem(f"acc_in{i}") for i in range(4)]
        gates_in = sem("gates_in")
        g_ready = sem("g_ready")
        o_done = sem("o_done")
        o_free = sem("o_free")
        x2_done = sem("x2_done")
        w2_scaled = sem("w2_scaled")
        ff_done = sem("ff_done")
        ff_relu = sem("ff_relu")
        ff_sq = sem("ff_sq")
        ff_hi_done = sem("ff_hi_done")
        ff_free = sem("ff_free")
        fin_in = sem("fin_in")
        y_out = sem("y_out")
        out_stored = [sem("out_stored0"), sem("out_stored1")]

        def released(c):
            kind, i = c
            if c in RELEASED_EARLY:
                return used, RELEASED_EARLY.index(c) + 1
            if kind in ("k", "v", "q", "g"):
                last = {"k": TILES, "v": VTILES, "q": range(NT), "g": range(NT)}[kind][-1]
                return main_done, MIDX[(kind, last)] + 1
            if kind == "u":
                return main_done, MIDX[("u", i, 1)] + 1
            if kind == "cs":
                return dft_done, i + 1
            if kind in ("ga", "gb", "fr"):
                return merge_done, 9 * i + {"ga": 2, "gb": 4, "fr": 9}[kind]
            return o_done, 8 * (i // 4 + 1)

        def slot(c):
            s = RIDX[c] % RING
            return ring_hi[:, s, :], ring_lo[:, s, :]

        def w1_slot(c):
            return (ring_hi[:, 2 + c, :], ring_lo[:, 2 + c, :]) if c < 2 else (x_hi[:, c - 2, :], x_lo[:, c - 2, :])

        def w2_slot(c):
            s = (0, 1, 4, 5)[c]
            return ring_hi[:, s, :], ring_lo[:, s, :]

        def main_wait(eng, i):
            if i >= 2:
                eng.wait_ge(main_free[i % 2], i // 2)

        def side_wait(eng, key):
            j = SIDX[key]
            if j >= 2:
                eng.wait_ge(side_free[j % 2], j // 2)

        def side_out(eng, key):
            j = SIDX[key]
            eng.wait_ge(side_free[j % 2], j // 2 + 1)

        def side_bank(key):
            return 2 + SIDX[key] % 2

        def h_tile(t):
            s = TILES.index(t)
            if s < 2:
                return hc_hi[:, :, s * P:(s + 1) * P], hc_lo[:, :, s * P:(s + 1) * P], s
            return hT_hi[:, :, t * P:(t + 1) * P], hT_lo[:, :, t * P:(t + 1) * P], s

        def x_tile(s):
            if s == 5:
                return ctx_in[:, 1, :]
            return ctx_in[:, s, :] if s < 2 else x_a[:, s - 2, :] if s < 5 else x_b[:, s - 6, :]

        class Steps:

            def __init__(self, eng, step):
                self.eng, self.step, self.count = eng, step, {}

            def __call__(self, ins, s=None):
                s = self.step if s is None else s
                ins.then_inc(s, 1)
                self.count[id(s)] = self.count.get(id(s), 0) + 1
                return self.count[id(s)]

            def chain(self, ins, s=None, value=None):
                n = self(ins, s)
                self.eng.wait_ge(self.step if s is None else s, n if value is None else value)

        block = ctx.enter_context(nc.Block())

        @block.sync
        def _(sp):
            for i, (kind, n) in enumerate(STREAM):
                if i >= 2:
                    sp.wait_ge(split, i - 1)
                dst = raw[:, i % 2, :]
                if kind in W_KINDS:
                    sp.dma_start(dst, ins["w_stream"][WIDX[(kind, n)]]).then_inc(raw_in[i % 2], 16)
                elif kind == "cs":
                    sp.dma_start(dst, ins["dft"][n]).then_inc(raw_in[i % 2], 16)
                elif kind == "y":
                    sp.wait_ge(y_stored, 16 * (n + 1))
                    sp.dma_start(dst, y_scr[n]).then_inc(raw_in[i % 2], 16)
                else:
                    sp.wait_ge(wpm_stored, 16 * KT)
                    sp.dma_start(dst[:, 0:512], wpm_scr[n]).then_inc(raw_in[i % 2], 16)
                    sp.dma_start(dst[:, 512:1024], ins["ret_stream"][n]).then_inc(raw_in[i % 2], 16)
            for c in range(FFB):
                i = MLP0 + c
                sp.wait_ge(split, i - 1)
                sp.dma_start(raw[:, i % 2, :], ins["w1_stream"][c]).then_inc(raw_in[i % 2], 16)

            def load_w2(b):
                for c in range(FFB):
                    i = MLP0 + FFB + c
                    sp.wait_ge(split, b * 8 + (i - 1))
                    sp.dma_start(raw[:, i % 2, :], ins["w2_stream"][b * FFB + c]).then_inc(raw_in[i % 2], 16)

            def load_next_w1(b):
                for c in range(FFB):
                    i = MLP0 + 8 + c
                    sp.wait_ge(split, b * 8 + (i - 1))
                    sp.dma_start(raw[:, i % 2, :], ins["w1_stream"][b * FFB + (FFB + c)]).then_inc(raw_in[i % 2], 16)

            with sp.Fori(0, BLOCKS - 1) as b:
                load_w2(b)
                load_next_w1(b)
            load_w2(BLOCKS - 1)
            for t in range(NT):
                sp.wait_ge(y_out, t + 1)
                sp.dma_start(out[t * P:(t + 1) * P, :], o_sb[:, t % 2, :]).then_inc(out_stored[t % 2], 16)
            for n in range(2):
                sp.wait_ge(out_stored[n], 16 * NT // 2)

        raw_seen = []
        landed = [0, 0]
        for i, (kind, n) in enumerate(STREAM):
            landed[i % 2] += 32 if kind == "fr" else 16
            raw_seen.append(landed[i % 2])
        raw_mlp = list(landed)

        def raw_wait(eng, i):
            eng.wait_ge(raw_in[i % 2], raw_seen[i])

        def raw_wait_mlp(eng, c, b):
            i = MLP0 + c
            k = c // 2 + 1
            eng.wait_ge(raw_in[i % 2], b * 64 + (raw_mlp[i % 2] + 16 * k))

        @block.gpsimd
        def _(pool):
            do = Steps(pool, pool_step)

            def lo(i):
                c = STREAM[i]
                if c[0] == "y":
                    hi_ap, lo_ap = yT_hi[:, c[1], :], yT_lo[:, c[1], :]
                else:
                    hi_ap, lo_ap = slot(c)
                pool.wait_ge(hi_done, i + 1)
                nc.gpsimd.tensor_tensor(lo_ap, raw[:, i % 2, :], hi_ap.bitcast(F32),
                                        ALU.subtract).then_inc(split, 1)

            def w_plus_minus(m, wp):
                if m:
                    pool.wait_ge(wpm_stored, 16 * m)
                pool.dma_start(wp[:], ins["four_stream"][m]).then_inc(wp_in, 16)
                pool.wait_ge(wp_in, 16 * (m + 1))
                part = wp[:, 1, :].rearrange("p (t c) -> p t c", t=4)
                do.chain(nc.gpsimd.tensor_tensor(part, part, coef[:, :, None].to_broadcast([P, 4, P]), ALU.mult))
                do.chain(nc.gpsimd.tensor_tensor(wp[:, 0, :], wp[:, 0, :], wp[:, 1, :], ALU.add))
                pool.dma_start(wpm_scr[m], wp[:, 0, :]).then_inc(wpm_stored, 16)

            for i in range(RING):
                lo(i)
            for n in range(10):
                hi_ap, lo_ap, _ = h_tile(TILES[n])
                pool.wait_ge(hhi_done, n + 1)
                for half in range(2):
                    side_out(pool, ("x", n, half))
                nc.gpsimd.tensor_tensor(lo_ap, h_f[:].rearrange("p (c t) -> p c t", c=KT), hi_ap.bitcast(F32),
                                        ALU.subtract).then_inc(h_ready, 1)
            for i in range(RING, INDEX[("q", 2)]):
                lo(i)
            pool.wait_ge(params_in, 16 * 4)
            pool.wait_ge(h_ready, 10)
            for m in range(4):
                w_plus_minus(m, wp_v)
            for i in range(INDEX[("q", 2)], INDEX[("u", 2)]):
                lo(i)
            pool.wait_ge(o_ready, NT)
            for m in range(4, 7):
                w_plus_minus(m, wp_g)
            for i in range(INDEX[("u", 2)], INDEX[("cs", 2)]):
                lo(i)
            w_plus_minus(7, wp_g)
            for i in range(INDEX[("cs", 2)], len(STREAM)):
                lo(i)

            def lo_mlp(c, b, hi_ap, lo_ap):
                i = MLP0 + c
                pool.wait_ge(hi_done, b * 8 + (i + 1))
                nc.gpsimd.tensor_tensor(lo_ap, raw[:, i % 2, :], hi_ap.bitcast(F32),
                                        ALU.subtract).then_inc(split, 1)

            def scale_w2(c, b):
                i = MLP0 + FFB + c
                raw_wait_mlp(pool, FFB + c, b)
                nc.gpsimd.tensor_tensor(raw[:, i % 2, :], raw[:, i % 2, :], g2b[:], ALU.mult).then_inc(w2_scaled, 1)

            for c in range(FFB):
                lo_mlp(c, 0, *w1_slot(c))
            pool.wait_ge(g_ready, 2)

            def block_w2(b):
                for c in range(FFB):
                    scale_w2(c, b)
                    lo_mlp(FFB + c, b, *w2_slot(c))

            with pool.Fori(0, BLOCKS - 1) as b:
                block_w2(b)
                for c in range(FFB):
                    lo_mlp(8 + c, b, *w1_slot(c))
            block_w2(BLOCKS - 1)

        @block.scalar
        def _(act):
            do = Steps(act, act_step)
            A = nc.scalar.activation

            def load(names, semaphore):
                for dst, name in names:
                    act.dma_start(dst[:], ins[name]).then_inc(semaphore, 16)

            def load_x(s):
                src = ins["ctx"][s * P:(s + 1) * P, :] if s < 2 else ins["x"][(s - 2) * P:(s - 1) * P, :]
                act.dma_start(x_tile(s), src).then_inc(x_landed[s], 16)

            def load_ada_rows(kt):
                act.dma_start(ada_in[:, kt, :], ins["w_ada"][kt * P:(kt + 1) * P, 0:2 * D]).then_inc(ada_landed[kt], 16)

            load(((cc, "cc"), (ident, "ident"), (gain1, "gain1"), (mod_rows, "b_rows")), first_in)
            load_x(0)
            load_ada_rows(0)
            load_ada_rows(1)
            load(((lgt, "logits"), (posc, "posc"), (dist, "dist")), decay_in)
            load_x(1)
            for kt in range(2, KT):
                load_ada_rows(kt)
            load_x(2)
            load_x(3)
            load(((gain2, "gain2"), (coef, "coef"), (bmod2, "bmod2"), (rope, "rope")), params_in)
            for s in (4, 6, 7, 8, 9):
                load_x(s)

            act.wait_ge(first_in, 16 * 4)
            A(silu_c[:], cc[:], ACT.Silu).then_inc(silu_done, 1)

            nhi = [0]

            def hi_to(key):
                while nhi[0] <= INDEX[key]:
                    i = nhi[0]
                    c = STREAM[i]
                    if c[0] == "y":
                        act.wait_ge(merge_done, 9 * 7 + 4)
                        dst = yT_hi[:, c[1], :]
                    else:
                        dst = slot(c)[0]
                        if RIDX[c] >= RING:
                            act.wait_ge(*released(RINGED[RIDX[c] - RING]))
                    raw_wait(act, i)
                    A(dst, raw[:, i % 2, :], ACT.Copy).then_inc(hi_done, 1)
                    nhi[0] += 1

            def copy_side(key, dst, src):
                act.wait_ge(side_done, SIDX[key] + 1)
                A(dst, src, ACT.Copy).then_inc(side_free[SIDX[key] % 2], 1)

            hi_to(("k", 1))

            def square(s):
                act.wait_ge(x_landed[s], 16)
                if s == 2:
                    act.wait_ge(rows_done, 4)
                if s:
                    act.wait_ge(sumsq, s)
                dst = junk[:] if s < 2 else ps[:, 4:6, :].rearrange("p a b -> p (a b)")
                A(dst, x_tile(s), ACT.Square, accum_out=ss[:, s:s + 1]).then_inc(sumsq, 1)

            def square_root(s):
                act.wait_ge(meansq, s + 1)
                A(rt[:, s:s + 1], ms[:, s:s + 1], ACT.Sqrt).then_inc(root, 1)

            square(0)
            square_root(0)
            act.wait_ge(decay_log, 1)
            A(lw[:, 1, :], lw[:, 0, :], ACT.Exp).then_inc(decay_exp, 1)
            act.wait_ge(decay_log, 2)
            A(lw[:, 3, :], lw[:, 2, :], ACT.Ln).then_inc(decay_exp, 1)
            act.wait_ge(decay_log, 3)
            A(dec[:], dec[:], ACT.Exp).then_inc(decay_exp, 1)
            for h in range(HEADS):
                if h:
                    act.wait_ge(decay_log, 3 + h)
                A(dtmp[:, 0, :], dist[:, 0, :], ACT.Exp, scale=lg[:, h:h + 1]).then_inc(decay_exp, 1)
                A(dtmp[:, 1, :], dist[:, 1, :], ACT.Exp, scale=lg[:, 8 + h:9 + h]).then_inc(decay_exp, 1)
            hi_to(("k", 3))
            square(1)
            square_root(1)
            hi_to(STREAM[RING - 1])
            for s in range(1, 13):
                if 2 <= s < 10:
                    square(s)
                    square_root(s)
                if s == 2:
                    act.wait_ge(side_done, SIDX[("x", 1, 1)] + 1)
                    load_x(5)
                if 1 <= s <= 10:
                    for half in range(2):
                        side_out(act, ("x", s - 1, half))
                    hi_ap, _, _ = h_tile(TILES[s - 1])
                    A(hi_ap, h_f[:].rearrange("p (c t) -> p c t", c=KT), ACT.Copy).then_inc(hhi_done, 1)
                if 2 <= s <= 3:
                    i = MIDX[("k", TILES[s - 2])]
                    act.wait_ge(main_done, i + 1)
                    A(k_c[:, s - 2, :], ps[:, i % 2, :], ACT.Copy).then_inc(main_free[i % 2], 1)
                if s == 12:
                    hi_to(("q", 1))
                if s >= 5:
                    t = s - 5
                    copy_side(("kt", t), kT[:, :, t * P:(t + 1) * P],
                              ps[:, side_bank(("kt", t)), :].rearrange("p (a j) -> p a j", a=PAIRS))

            for j, t in enumerate(range(NT - 1, -1, -1)):
                if t == 5:
                    act.wait_ge(kvc_done, 1)
                if t == 0:
                    hi_to(("q", 3))
                i = MIDX[("v", t)]
                act.wait_ge(main_done, i + 1)
                A(v[:, t, :], ps[:, i % 2, :], ACT.Copy).then_inc(main_free[i % 2], 1)
                if t == 0:
                    hi_to(("g", 1))
                if j:
                    copy_side(("kv", t + 1), kv[:, t + 1, :], ps[:, side_bank(("kv", t + 1)), :])
            copy_side(("kv", 0), kv[:, 0, :], ps[:, side_bank(("kv", 0)), :])

            for j in range(1, 17):
                if j == 7:
                    hi_to(("g", 3))
                if j == 9:
                    hi_to(("u", 1))
                if j == 16:
                    hi_to(("cs", 1))
                if j <= 8:
                    t = j - 1
                    copy_side(("qt", t), qT[:, :, t * P:(t + 1) * P],
                              ps[:, side_bank(("qt", t)), :].rearrange("p (a j) -> p a j", a=PAIRS))
                if j >= 8 and j - 8 < NT:
                    n = j - 8
                    i = MIDX[("g", n)]
                    if n == 0:
                        act.wait_ge(roped, 2 * NT)
                        act.dma_start(gnb[:], ins["gn_rows"]).then_inc(late_in, 16)
                    if n >= 2:
                        act.wait_ge(r_ready, n - 1)
                    act.wait_ge(main_done, i + 1)
                    A(sg[:, n % 2, :], ps[:, i % 2, :], ACT.Silu).then_inc(silu_g, 1)
                if 3 <= j <= 10:
                    n = j - 3
                    act.wait_ge(meansq, 10 + n + 1)
                    A(hss[:, :, 2], hss[:, :, 1], ACT.Sqrt).then_inc(root, 1)
                if j == 12:
                    act.wait_ge(masked, 2 * NT)
                    act.dma_start(mcs[:], ins["mcs"]).then_inc(late_in, 16)
                    act.dma_start(sgn[:], ins["sgn"]).then_inc(late_in, 16)

            for g in range(GROUPS):
                i = MIDX[("u", g, 0)]
                act.wait_ge(main_done, i + 1)
                if g:
                    act.wait_ge(ue_ready, g)
                else:
                    act.wait_ge(r_ready, NT)
                A(u_lo[:], ps[:, 0, :], ACT.Copy).then_inc(main_free[0], 1)
                if g == 3:
                    hi_to(("cs", 3))
            hi_to(("gb", 1))
            act.wait_ge(dft_done, 4)
            act.dma_start(wn_raw[:], ins["four_nyq"]).then_inc(wn_in, 16)

            def store_y(m):
                act.wait_ge(y_ready, m + 1)
                act.dma_start(y_scr[m], y[:]).then_inc(y_stored, 16)

            def row_out(a, banks):
                for half in range(2):
                    act.wait_ge(ada_red, 2 * a + half + 1)
                    if a or half:
                        act.wait_ge(row_stored, 16 * (2 * a + half))
                    A(ada_row[:], ps[0:1, banks + half, :], ACT.Copy).then_inc(ada_row_out, 1)
                    act.wait_ge(ada_row_out, 2 * a + half + 1)
                    act.dma_start(mod_scr[a:a + 1, half * 512:(half + 1) * 512], ada_row[:]).then_inc(row_stored, 16)

            def load_ada(j):
                if j:
                    act.wait_ge(ada_acc_done, j)
                act.dma_start(ada_raw[:], ins["w_ada"][(j % 8) * P:(j % 8 + 1) * P, (2 + j // 8) * D:(3 + j // 8) * D]
                              ).then_inc(ada_raw_in, 16)

            for m in range(KT):
                load_ada(4 * m)
                if m + 1 < KT:
                    hi_to(("fr", m + 1))
                act.wait_ge(merge_done, 9 * m + 2)
                if m:
                    act.wait_ge(y_ready, m)
                A(sig_a[:], ps[:, 0:2, :].rearrange("p a b -> p (a b)"), ACT.Sigmoid).then_inc(gates_done, 1)
                load_ada(4 * m + 1)
                hi_to(("ga", m + 2) if m + 2 < KT else ("wo", 2 * (m - 6)))
                load_ada(4 * m + 2)
                if m:
                    store_y(m - 1)
                act.wait_ge(merge_done, 9 * m + 4)
                A(sig_b[:], ps[:, 2:4, :].rearrange("p a b -> p (a b)"), ACT.Sigmoid).then_inc(gates_done, 1)
                load_ada(4 * m + 3)
                if m in (2, 4, 6):
                    row_out(m // 2 - 1, 6)
                hi_to(("gb", m + 2) if m + 2 < KT else ("wo", 2 * (m - 6) + 1))
            hi_to(("y", 6))
            row_out(3, 2)
            hi_to(("wo", 4))
            act.wait_ge(merge_done, 9 * KT)
            for n in range(4):
                act.dma_start(acc[:, 2 * n:2 * n + 2, :],
                              ins["x"][2 * n * P:(2 * n + 2) * P, :].rearrange("(t p) d -> p t d", p=P)
                              ).then_inc(acc_in[n], 16)
            act.wait_ge(y7_ready, 1)
            act.wait_ge(row_stored, 16 * 8)
            act.dma_start(g1b[:], mod_scr[0:1, :].to_broadcast([P, D])).then_inc(gates_in, 16)
            act.dma_start(g2b[:], mod_scr[3:4, :].to_broadcast([P, D])).then_inc(gates_in, 16)
            act.dma_start(b1b[:], ins["b_ada"][:, 2 * D:3 * D].to_broadcast([P, D])).then_inc(gates_in, 16)
            act.dma_start(b2b[:], ins["b_ada"][:, 5 * D:6 * D].to_broadcast([P, D])).then_inc(gates_in, 16)
            with nc.allow_non_contiguous_dma(reason="2048 modulation values, one per row"):
                for a in range(2):
                    act.dma_start(mod2[:, a, :], mod_scr[1 + a, :].rearrange("(c p) -> p c", p=P)).then_inc(gates_in, 16)
            hi_to(("wo", 7))

            def hi_mlp(c, b, dst):
                raw_wait_mlp(act, c, b)
                A(dst, raw[:, (MLP0 + c) % 2, :], ACT.Copy).then_inc(hi_done, 1)

            for c in range(FFB):
                if c < 2:
                    act.wait_ge(*released(("wo", 2 + c)))
                elif c == 2:
                    act.wait_ge(g_ready, 3)
                hi_mlp(c, 0, w1_slot(c)[0])

            for t in range(NT + 2):
                if t < NT:
                    act.wait_ge(x2_done, t + 1)
                    act.wait_ge(sumsq, 10 + t)
                    A(junk2[:], acc[:, t, :], ACT.Square, accum_out=ss[:, t:t + 1]).then_inc(sumsq, 1)
                if t >= 2:
                    for half in range(2):
                        side_out(act, ("z", t - 2, half))
                    A(h2_hi[:, :, (t - 2) * P:(t - 1) * P], h2_f[:].rearrange("p (c t) -> p c t", c=KT),
                      ACT.Copy).then_inc(hhi_done, 1)
                if t < NT:
                    act.wait_ge(meansq, 18 + t + 1)
                    A(rt[:, t:t + 1], ms[:, t:t + 1], ACT.Sqrt).then_inc(root, 1)

            def relu_square(f, b):
                act.wait_ge(ff_done, b * 8 + (f + 1))
                A(ps[:, f % 2, :], ps[:, f % 2, :], ACT.Relu).then_inc(ff_relu, 1)
                act.wait_ge(ff_relu, b * 8 + (f + 1))
                A(ps[:, f % 2, :], ps[:, f % 2, :], ACT.Square).then_inc(ff_sq, 1)

            def mlp_block(b, last):
                for f in range(8):
                    if f < FFB:
                        if f == 0:
                            act.wait_ge(o_done, b * 16 + 16)
                        act.wait_ge(w2_scaled, b * FFB + (f + 1))
                        hi_mlp(FFB + f, b, w2_slot(f)[0])
                    relu_square(f, b)
                    if f >= FFB and not last:
                        act.wait_ge(ff_done, b * 8 + (f + 1))
                        hi_mlp(4 + f, b, w1_slot(f - FFB)[0])

            with act.Fori(0, BLOCKS - 1) as b:
                mlp_block(b, False)
            mlp_block(BLOCKS - 1, True)
            act.wait_ge(ff_done, 8 * BLOCKS)
            act.dma_start(fgb[:], ins["final_gain"].to_broadcast([P, D])).then_inc(fin_in, 16)
            for t in range(NT):
                act.wait_ge(o_free, 16 * BLOCKS + 2 * t + 2)
                act.wait_ge(sumsq, 18 + t)
                A(junk3[:], acc[:, t, :], ACT.Square, accum_out=ss[:, t:t + 1]).then_inc(sumsq, 1)
                act.wait_ge(meansq, 26 + t + 1)
                A(rt[:, t:t + 1], ms[:, t:t + 1], ACT.Sqrt).then_inc(root, 1)

        @block.vector
        def _(dve):
            do = Steps(dve, dve_step)
            V = nc.vector

            def mean_root(src, dst_m, n, src_r, dst_r, count_in, count_root):
                dve.wait_ge(sumsq, count_in)
                V.tensor_scalar(dst_m, src, 1.0 / n, EPS, ALU.mult, ALU.add).then_inc(meansq, 1)
                dve.wait_ge(root, count_root)
                do.chain(V.reciprocal(dst_r, src_r))

            def tokens_norm(s):
                mean_root(ss[:, s:s + 1], ms[:, s:s + 1], D, rt[:, s:s + 1], rstd[:, s:s + 1], s + 1, s + 1)
                V.tensor_scalar(x_tile(s), x_tile(s), rstd[:, s:s + 1], None, ALU.mult).then_inc(xhat, 1)

            V.memset(ones[:], 1.0).then_inc(mod_ready, 1)
            tokens_norm(0)
            dve.wait_ge(decay_in, 16 * 3)
            do.chain(V.tensor_scalar(lw[:, 0, :], lgt[:], -1.0, None, ALU.mult))
            do.chain(V.tensor_tensor(lw[:, 0, :], lw[:, 0, :], lgt[:], ALU.min), decay_log)
            dve.wait_ge(decay_exp, 1)
            do.chain(V.tensor_scalar(lw[:, 2, :], lw[:, 1, :], 1.0, None, ALU.add), decay_log)
            do(V.reciprocal(lw[:, 5, :], lw[:, 2, :]))
            do.chain(V.tensor_scalar(lw[:, 4, :], lw[:, 2, :], -1.0, None, ALU.add))
            do.chain(V.tensor_tensor(lw[:, 4, :], lw[:, 1, :], lw[:, 4, :], ALU.subtract))
            do.chain(V.tensor_tensor(lw[:, 4, :], lw[:, 4, :], lw[:, 5, :], ALU.mult))
            dve.wait_ge(decay_exp, 2)
            do.chain(V.tensor_tensor(lw[:, 4, :], lw[:, 4, :], lw[:, 3, :], ALU.add))
            do.chain(V.tensor_scalar(lg[:], lgt[:], 0.0, None, ALU.min))
            do.chain(V.tensor_tensor(lg[:], lg[:], lw[:, 4, :], ALU.subtract))
            do.chain(V.tensor_tensor(dec[:], posc[:], lg[:, None, :].to_broadcast([P, 5, 16]), ALU.mult), decay_log)
            dve.wait_ge(decay_exp, 3)
            do.chain(V.tensor_scalar(dec[:, 1:4, :], dec[:, 1:4, :], HD ** -0.5, None, ALU.mult))
            pair_dec = dec[:, 4, :].rearrange("p (d a e) -> p a d e", d=2, e=2)
            do(V.tensor_copy(dec_s[0:64], pair_dec[0:64, :, :, 0]))
            do(V.tensor_copy(dec_s[64:128], pair_dec[64:128, :, :, 1]))
            for h in range(HEADS):
                dve.wait_ge(decay_exp, 3 + 2 * (h + 1))
                do(V.tensor_tensor(dmask[:, h, :], dtmp[:, 0, :], dist[:, 2, :], ALU.mult))
                do.chain(V.tensor_tensor(dtmp[:, 2, :], dtmp[:, 1, :], dist[:, 3, :], ALU.mult), decay_log)
                do.chain(V.tensor_tensor(dmask[:, h, :], dmask[:, h, :], dtmp[:, 2, :], ALU.add))

            tokens_norm(1)

            def modulate(a, sh, keys):
                for half, key in enumerate(keys):
                    dve.wait_ge(side_done, SIDX[key] + 1)
                    if half == 0 and h_written[0]:
                        dve.wait_ge(*h_written[0])
                    for q in range(4):
                        c = 4 * half + q
                        ins_ = V.tensor_scalar(h_dst[0][:, c * P:(c + 1) * P],
                                               ps[:, side_bank(key), q * P:(q + 1) * P],
                                               a(c), sh(c), ALU.mult, ALU.add)
                    ins_.then_inc(side_free[SIDX[key] % 2], 1)

            h_dst = [h_f]
            h_written = [None]

            dve.wait_ge(first_in, 16 * 4)
            for q in range(4):
                dve.wait_ge(ada_done, 1)
                V.tensor_tensor(mod_rows[:, q * 512:(q + 1) * 512], ps[0:2, 4 + q, :],
                                mod_rows[:, q * 512:(q + 1) * 512], ALU.add).then_inc(rows_done, 1)
            dve.wait_ge(modT_done, 1)
            do.chain(V.tensor_copy(mod[:], ps[:, 0, 0:32].rearrange("p (c r) -> p c r", r=2)))
            do.chain(V.tensor_scalar(a1[:], mod[:, KT:2 * KT, :], 1.0, None, ALU.add))
            V.tensor_tensor(a1[:], a1[:], gain1[:, :, None].to_broadcast([P, KT, 2]), ALU.mult).then_inc(mod_ready, 1)
            dve.wait_ge(mod_ready, 2)

            def rope_tile(src, t, dst, ta, tb, i):
                sv = src.rearrange("p (h e f) -> p h e f", h=HEADS, e=2)
                dv = dst.rearrange("p (h e f) -> p h e f", h=HEADS, e=2)
                av = ta.rearrange("p (h e f) -> p h e f", h=HEADS, e=2)
                bv = tb.rearrange("p (h e f) -> p h e f", h=HEADS, e=2)
                cos = rope[:, t, 0, :][:, None, :].to_broadcast([P, 2 * HEADS, HD // 2])
                sin = rope[:, t, 1, :][:, None, :].to_broadcast([P, 2 * HEADS, HD // 2])
                dve.wait_ge(main_done, i + 1)
                do(V.tensor_tensor(ta.rearrange("p (h f) -> p h f", f=HD // 2),
                                   src.rearrange("p (h f) -> p h f", f=HD // 2), cos, ALU.mult))
                do.chain(V.tensor_tensor(tb.rearrange("p (h f) -> p h f", f=HD // 2),
                                         src.rearrange("p (h f) -> p h f", f=HD // 2), sin, ALU.mult),
                         main_free[i % 2], i // 2 + 1)
                do(V.tensor_tensor(dv[:, :, 0, :], av[:, :, 0, :], bv[:, :, 1, :], ALU.subtract))
                do.chain(V.tensor_tensor(dv[:, :, 1, :], av[:, :, 1, :], bv[:, :, 0, :], ALU.add), roped)

            dve.wait_ge(params_in, 16 * 4)
            for s in range(1, 12):
                if 2 <= s < 10:
                    tokens_norm(s)
                if 1 <= s <= 10:
                    n = s - 1
                    r = 1 if n < 2 else 0
                    modulate(lambda c: a1[:, c, r:r + 1], lambda c: mod[:, c, r:r + 1], [("x", n, 0), ("x", n, 1)])
                    h_written[0] = (h_ready, n + 1)
                if s >= 4:
                    t = s - 4
                    i = MIDX[("k", t)]
                    rope_tile(ps[:, i % 2, :], t, kv[:, t, :], t1[:, 0, :], t1[:, 1, :], i)

            def v_decayed(dst, src, r, d):
                g = dec[:, r, 8 * d:8 * d + 8][:, :, None].to_broadcast([P, HEADS, HD])
                return V.tensor_tensor(dst.rearrange("p (h d v) -> p h d v", h=HEADS, d=2)[:, :, d, :],
                                       src.rearrange("p (h v) -> p h v", h=HEADS), g, ALU.mult)

            def roll_state(cur, other, d, t, signal=None):
                g = dec_s[:, :, d][:, :, None].to_broadcast([P, PAIRS, HD])
                kvt = kv[:, t, :].rearrange("p (a d v) -> p a d v", a=PAIRS, d=2)[:, :, d, :]
                do.chain(V.tensor_tensor(other, cur, g, ALU.mult))
                do.chain(V.tensor_tensor(other, other, kvt, ALU.add))
                do.chain(V.tensor_copy(kvt, cur), signal)

            for r in range(2):
                i = MIDX[("v", VTILES[r])]
                dve.wait_ge(main_done, i + 1)
                do(v_decayed(vcat_c[:, r, :], ps[:, i % 2, :], 2 + r, 0), vcat_ready)
                do(v_decayed(vcat_c[:, r, :], ps[:, i % 2, :], 2 + r, 1), main_free[i % 2])
            dve.wait_ge(kvc_done, 1)
            bank7 = ps[:, 7, :].rearrange("p (a d v) -> p a d v", a=PAIRS, d=2)
            cur_b, oth_b = st_b[:, 0], st_b[:, 1]
            do.chain(V.tensor_copy(cur_b, bank7[:, :, 1, :]))
            for j, t in enumerate(range(NT - 1, -1, -1)):
                i = MIDX[("v", t)]
                dve.wait_ge(main_free[i % 2], i // 2 + 1)
                if j >= 2:
                    side_out(dve, ("kv", t + 2))
                for d in range(2):
                    do(v_decayed(vcat[:, j % 2, :], v[:, t, :], 1, d), vcat_ready)
                if j >= 2:
                    roll_state(cur_b, oth_b, 1, t + 2)
                    cur_b, oth_b = oth_b, cur_b
            side_out(dve, ("kv", 1))
            roll_state(cur_b, oth_b, 1, 1)
            cur_b, oth_b = oth_b, cur_b
            side_out(dve, ("kv", 0))
            do.chain(V.tensor_copy(kv[:, 0, :].rearrange("p (a d v) -> p a d v", a=PAIRS, d=2)[:, :, 1, :], cur_b))
            dve.wait_ge(wpm_stored, 16 * 4)
            cur_f, oth_f = st_f[:, 0], st_f[:, 1]
            do.chain(V.tensor_copy(cur_f, bank7[:, :, 0, :]))

            def split_side(n):
                key = ("rt", n)
                dve.wait_ge(side_done, SIDX[key] + 1)
                src = ps[:, side_bank(key), :].rearrange("p (a t) -> p a t", a=PAIRS)
                h_ap, l_ap = rT_hi[:, :, n * P:(n + 1) * P], rT_lo[:, :, n * P:(n + 1) * P]
                do.chain(V.tensor_copy(h_ap, src))
                do(V.tensor_tensor(l_ap, src, h_ap.bitcast(F32), ALU.subtract), side_free[SIDX[key] % 2])

            for j in range(18):
                if 1 <= j <= 8:
                    t = j - 1
                    if t < NT - 1:
                        roll_state(cur_f, oth_f, 0, t, states_ready)
                        cur_f, oth_f = oth_f, cur_f
                    else:
                        do.chain(V.tensor_copy(kv[:, t, :].rearrange("p (a d v) -> p a d v", a=PAIRS, d=2)[:, :, 0, :],
                                               cur_f), states_ready)
                    if t >= 1:
                        dve.wait_ge(side_done, SIDX[("qt", t - 1)] + 1)
                    rope_tile(ps[:, MIDX[("q", t)] % 2, :], t, qa[:], qa[:], qb[:], MIDX[("q", t)])
                if 3 <= j <= 10:
                    n = j - 3
                    dve.wait_ge(inter_done, n + 1)
                    dve.wait_ge(intra_done, n + 1)
                    ov = v[:, n, :].rearrange("p (a e v) -> p a e v", a=PAIRS, e=2)
                    for e in range(2):
                        src = ps[:, 6 + e, :].rearrange("p (a d v) -> p a d v", a=PAIRS, d=2)
                        dq = dec[:, 0, :].rearrange("p (d a e) -> p a d e", d=2, e=2)[:, :, :, e]
                        do.chain(V.tensor_tensor(it[:], src, dq[:, :, :, None].to_broadcast([P, PAIRS, 2, HD]),
                                                 ALU.mult))
                        do.chain(V.tensor_tensor(ov[:, :, e, :], it[:, :, 0, :], it[:, :, 1, :], ALU.add))
                        own = ps[:, 4 + e, :].rearrange("p (a e v) -> p a e v", a=PAIRS, e=2)[:, :, e, :]
                        if e == 0:
                            do.chain(V.tensor_tensor(ov[:, :, e, :], ov[:, :, e, :], own, ALU.add))
                        else:
                            do.chain(V.tensor_tensor(ov[:, :, e, :], ov[:, :, e, :], own, ALU.add), combined)
                    do.chain(V.tensor_tensor(sq[:], v[:, n, :], v[:, n, :], ALU.mult))
                    do.chain(V.tensor_reduce(hss[:, :, 0], sq[:].rearrange("p (h v) -> p h v", h=HEADS), AX.X,
                                             ALU.add))
                    V.tensor_scalar(hss[:, :, 1], hss[:, :, 0], 1.0 / HD, EPS, ALU.mult, ALU.add).then_inc(meansq, 1)
                    dve.wait_ge(root, 10 + n + 1)
                    do.chain(V.reciprocal(hss[:, :, 3], hss[:, :, 2]))
                    do.chain(V.tensor_tensor(v[:, n, :].rearrange("p (h v) -> p h v", h=HEADS),
                                             v[:, n, :].rearrange("p (h v) -> p h v", h=HEADS),
                                             hss[:, :, 3:4].to_broadcast([P, HEADS, HD]), ALU.mult), o_ready)
                if 2 <= j <= 9:
                    n = j - 2
                    dve.wait_ge(scores_done, n + 1)
                    if n:
                        dve.wait_ge(intra_done, n)
                    for e in range(2):
                        src = ps[:, 4 + e, :].rearrange("p (a i) -> p a i", a=PAIRS)
                        av = aT[:].rearrange("p (a e) i -> p a e i", e=2)[:, :, e, :]
                        mv = dmask[:].rearrange("p (a e) i -> p a e i", e=2)[:, :, e, :]
                        V.tensor_tensor(av, src, mv, ALU.mult).then_inc(masked, 1)
                if 9 <= j < 17:
                    n = j - 9
                    if n == 0:
                        dve.wait_ge(late_in, 16)
                    i = MIDX[("g", n)]
                    dve.wait_ge(silu_g, n + 1)
                    do.chain(V.tensor_tensor(v[:, n, :], v[:, n, :], gnb[:], ALU.mult), main_free[i % 2], i // 2 + 1)
                    do.chain(V.tensor_tensor(v[:, n, :], v[:, n, :], sg[:, n % 2, :], ALU.mult), r_ready)
                if j >= 11:
                    split_side(j - 11)
            split_side(7)

            dve.wait_ge(late_in, 48)
            for g in range(GROUPS):
                i = MIDX[("u", g, 1)]
                dve.wait_ge(main_free[0], MIDX[("u", g, 0)] // 2 + 1)
                dve.wait_ge(main_done, i + 1)
                up = ps[:, i % 2, :]
                back = up[:, HALF - 1:0:-1]
                do(V.tensor_tensor(u_e[:, g, 1:HALF], u_lo[:, 1:HALF], back, ALU.add))
                do(V.tensor_copy(u_e[:, g, 0:1], u_lo[:, 0:1]))
                do(V.memset(u_o[:, g, 0:1], 0.0))
                do(V.tensor_copy(u_c[:, 0, g:g + 1], up[:, 0:1]))
                do.chain(V.tensor_tensor(u_o[:, g, 1:HALF], u_lo[:, 1:HALF], back, ALU.subtract), main_free[1], i // 2 + 1)
                do.chain(V.tensor_tensor_reduce(fj[:], u_e[:, g, :], sgn[:], 1.0, 0.0, ALU.mult, ALU.add,
                                                u_c[:, 1, g:g + 1]), ue_ready)
            V.scalar_tensor_tensor(u_c[:, 1, :], u_c[:, 0, :], SEQ ** -0.5, u_c[:, 1, :], ALU.mult,
                                   ALU.add).then_inc(uc_ready, 1)

            for nt in range(4):
                for part in range(2):
                    b = 4 + 2 * (nt % 2) + part
                    dve.wait_ge(pq_done, 2 * nt + part + 1)
                    src = ps[:, b, :].rearrange("p (g d) -> p g d", g=GROUPS)
                    if part == 0:
                        do.chain(V.tensor_copy(pn_hi[:, nt, :], src[:, :, 64]))
                        do(V.tensor_tensor(pn_lo[:, nt, :], src[:, :, 64], pn_hi[:, nt, :].bitcast(F32), ALU.subtract))
                    h_ap, l_ap = ((pa_hi, pa_lo), (pb_hi, pb_lo))[part]
                    hv = h_ap[:, nt, :].rearrange("p (g d) -> p g d", g=GROUPS)
                    lv = l_ap[:, nt, :].rearrange("p (g d) -> p g d", g=GROUPS)
                    do.chain(V.tensor_copy(hv, src[:, :, 0:64]))
                    do(V.tensor_tensor(lv, src[:, :, 0:64], hv.bitcast(F32), ALU.subtract), pq_free)
                if nt == 0:
                    dve.wait_ge(cols_done, 1)
                    do.chain(V.tensor_copy(cols[:], ps[:, 3, 0:4].rearrange("p (a r) -> p a r", a=2)))
                    do.chain(V.tensor_copy(cols_n[:], ps[0:GROUPS, 3, 4:8]), cols_free)
                    do.chain(V.tensor_copy(a5_hi[:, :, 0], cols[:, :, 1]))
                    do.chain(V.tensor_copy(a5_hi[:, :, 1], cols[:, :, 1]))
                    do(V.tensor_tensor(a5_lo[:, :, 0], cols[:, :, 1], a5_hi[:, :, 0].bitcast(F32), ALU.subtract))
                    do(V.tensor_tensor(a5_lo[:, :, 1], cols[:, :, 1], a5_hi[:, :, 0].bitcast(F32), ALU.subtract))
                    for q in range(2):
                        do.chain(V.tensor_copy(n5_hi[:, q:q + 1], cols_n[:, 2:3]))
                        do(V.tensor_tensor(n5_lo[:, q:q + 1], cols_n[:, 2:3], n5_hi[:, q:q + 1].bitcast(F32),
                                           ALU.subtract))

            dve.wait_ge(dft_done, 4)
            for p in range(2):
                do.chain(V.scalar_tensor_tensor(ft[:], sgn[:], cols[:, p, 0:1], ps[:, p, :], ALU.mult, ALU.add))
                do.chain(V.tensor_copy(ab_hi[:, p, :], ft[:]))
                do.chain(V.tensor_tensor(ab_lo[:, p, :], ft[:], ab_hi[:, p, :].bitcast(F32), ALU.subtract), ab_ready)
            for p in range(2):
                do.chain(V.tensor_copy(ab_hi[:, 2 + p, :], ps[:, 2 + p, :]))
                do.chain(V.tensor_tensor(ab_lo[:, 2 + p, :], ps[:, 2 + p, :], ab_hi[:, 2 + p, :].bitcast(F32),
                                         ALU.subtract), ab_ready)
            dve.wait_ge(wpm_stored, 16 * KT)
            do.chain(V.scalar_tensor_tensor(ft[0:GROUPS, :], sgn[0:GROUPS, :], cols_n[:, 0:1], ps[0:GROUPS, 4, :],
                                            ALU.mult, ALU.add))
            do.chain(V.tensor_copy(an_hi[:], ft[0:GROUPS, :]))
            do.chain(V.tensor_tensor(an_lo[:], ft[0:GROUPS, :], an_hi[:].bitcast(F32), ALU.subtract), ab_ready)
            dve.wait_ge(wn_in, 16)
            do.chain(V.tensor_copy(wn_hi[:], wn_raw[:]))
            do.chain(V.tensor_tensor(wn_lo[:], wn_raw[:], wn_hi[:].bitcast(F32), ALU.subtract), ab_ready)

            for m in range(KT):
                for a in range(4):
                    jj = 4 * m + a
                    kt = jj % 8
                    dve.wait_ge(ada_raw_in, 16 * (jj + 1))
                    if kt == 0:
                        if jj:
                            dve.wait_ge(ada_red, 2 * (jj // 8))
                        do.chain(V.tensor_scalar(ada_acc[:], ada_raw[:], silu_c[:, 0, 0:1], None, ALU.mult),
                                 ada_acc_done)
                    else:
                        do.chain(V.scalar_tensor_tensor(ada_acc[:], ada_raw[:], silu_c[:, kt, 0:1], ada_acc[:],
                                                        ALU.mult, ALU.add), ada_acc_done)
                dve.wait_ge(merge_done, 9 * m + 7)
                if m:
                    dve.wait_ge(y_stored, 16 * m)
                do.chain(V.tensor_copy(b_sb[:], ps[:, 5, :]))
                do(V.tensor_tensor(y[:, 0:HALF], ps[:, 4, :], b_sb[:], ALU.subtract))
                do(V.tensor_tensor(y[:, SEQ - 1:HALF:-1], ps[:, 4, 1:HALF], b_sb[:, 1:HALF], ALU.add), four_free)
                do.chain(V.tensor_copy(y[:, HALF:HALF + 1], ps[:, 0, 0:1]), col_free)
                dve.wait_ge(gates_done, 2 * m + 2)
                do.chain(V.tensor_tensor(y[:], y[:], sig_a[:], ALU.mult))
                dve.wait_ge(merge_done, 9 * m + 9)
                do.chain(V.tensor_tensor(sig_b[:], sig_b[:], ps[:, 6:8, :].rearrange("p a b -> p (a b)"), ALU.mult),
                         ret_free)
                do.chain(V.tensor_tensor(y[:], y[:], sig_b[:], ALU.add), y_ready)
                if m == KT - 1:
                    do.chain(V.tensor_copy(yT_hi[:, m, :], y[:]))
                    V.tensor_tensor(yT_lo[:, m, :], y[:], yT_hi[:, m, :].bitcast(F32), ALU.subtract).then_inc(y7_ready, 1)
                    dve.wait_ge(y7_ready, 1)

            dve.wait_ge(gates_in, 16 * 6)
            do.chain(V.tensor_tensor(g1b[:], g1b[:], b1b[:], ALU.add), g_ready)
            do.chain(V.tensor_tensor(g2b[:], g2b[:], b2b[:], ALU.add), g_ready)
            do.chain(V.tensor_tensor(mod2[:], mod2[:], bmod2[:], ALU.add))
            do.chain(V.tensor_scalar(a2[:], mod2[:, 1, :], 1.0, None, ALU.add))
            do.chain(V.tensor_tensor(a2[:], a2[:], gain2[:], ALU.mult), g_ready)

            def residual(nh, t):
                i = nh * NT + t
                if nh == 0 and t % 2 == 0:
                    dve.wait_ge(acc_in[t // 2], 16)
                dve.wait_ge(o_done, i + 1)
                do.chain(V.tensor_tensor(gated[:], ps[:, 4 + i % 4, :], g1b[:, nh * 512:(nh + 1) * 512], ALU.mult),
                         o_free)
                dst = acc[:, t, nh * 512:(nh + 1) * 512]
                do.chain(V.tensor_tensor(dst, dst, gated[:], ALU.add), x2_done if nh else None)

            do.chain(V.memset(rt[:, 15:16], 0.0), ff_free)
            do.chain(V.memset(rt[:, 15:16], 0.0), ff_free)
            for t in range(NT):
                residual(0, t)
            h_dst[0] = h2_f
            h_written[0] = None
            for t in range(NT + 2):
                if 1 <= t <= NT:
                    u = t - 1
                    mean_root(ss[:, u:u + 1], ms[:, u:u + 1], D, rt[:, u:u + 1], rstd[:, u:u + 1],
                              10 + u + 1, 18 + u + 1)
                    if u >= 2:
                        dve.wait_ge(side_done, SIDX[("z", u - 2, 1)] + 1)
                    V.tensor_scalar((xh, xh_b)[u % 2][:], acc[:, u, :], rstd[:, u:u + 1], None,
                                    ALU.mult).then_inc(xhat, 1)
                if t < NT:
                    residual(1, t)
                if t >= 2:
                    u = t - 2
                    modulate(lambda c: a2[:, c:c + 1], lambda c: mod2[:, 0, c:c + 1], [("z", u, 0), ("z", u, 1)])
                    dve.wait_ge(hhi_done, 10 + u + 1)
                    V.tensor_tensor(h2_lo[:, :, u * P:(u + 1) * P], h2_f[:].rearrange("p (c t) -> p c t", c=KT),
                                    h2_hi[:, :, u * P:(u + 1) * P].bitcast(F32), ALU.subtract).then_inc(h_ready, 1)
                    h_written[0] = (h_ready, 10 + u + 1)
            dve.wait_ge(h_ready, 18)

            def split_ff(f, b):
                dve.wait_ge(ff_sq, b * 8 + (f + 1))
                dve.wait_ge(o_done, b * 16 + 16)
                half, c = f // FFB, f % FFB
                h_ap, l_ap = ff_hi[:, c, half * 512:(half + 1) * 512], ff_lo[:, c, half * 512:(half + 1) * 512]
                V.tensor_copy(h_ap, ps[:, f % 2, :]).then_inc(ff_hi_done, 1)
                dve.wait_ge(ff_hi_done, b * 8 + (f + 1))
                V.tensor_tensor(l_ap, ps[:, f % 2, :], h_ap.bitcast(F32), ALU.subtract).then_inc(ff_free, 1)

            def add_out(i, b):
                t, nh = i // 2, i % 2
                dst = acc[:, t, nh * 512:(nh + 1) * 512]
                dve.wait_ge(o_done, b * 16 + (16 + i + 1))
                dve.wait_ge(o_free, b * 16 + (i + 1))
                V.tensor_tensor(dst, ps[:, 4 + i % 4, :], dst, ALU.add).then_inc(o_free, 1)

            with dve.Fori(0, BLOCKS - 1) as b:
                for f in range(8):
                    split_ff(f, b)
                for i in range(16):
                    add_out(i, b)
            b = BLOCKS - 1
            for f in range(8):
                split_ff(f, b)

            def final(t):
                mean_root(ss[:, t:t + 1], ms[:, t:t + 1], D, rt[:, t:t + 1], rstd[:, t:t + 1], 18 + t + 1, 26 + t + 1)
                if t == 0:
                    dve.wait_ge(fin_in, 16)
                if t >= 2:
                    dve.wait_ge(out_stored[t % 2], 16 * (t // 2))
                V.scalar_tensor_tensor(o_sb[:, t % 2, :], acc[:, t, :], rstd[:, t:t + 1], fgb[:], ALU.mult,
                                       ALU.mult).then_inc(y_out, 1)

            for t in range(NT):
                add_out(2 * t, b)
                add_out(2 * t + 1, b)
                if t:
                    final(t - 1)
            final(NT - 1)

        @block.tensor
        def _(pe):
            M = nc.tensor.matmul

            def mm3(dst, l_hi, l_lo, r_hi, r_lo, first, last):
                M(dst, lhsT=l_hi, rhs=r_hi, start=first, stop=False)
                M(dst, lhsT=l_hi, rhs=r_lo, start=False, stop=False)
                return M(dst, lhsT=l_lo, rhs=r_hi, start=False, stop=last)

            def chunk(c):
                pe.wait_ge(split, INDEX[c] + 1)
                return slot(c)

            def token_major(last_tile, kind, dst, l_hi, l_lo, middle):
                for kp in range(4):
                    c = (kind, kp)
                    r_hi, r_lo = chunk(c)
                    for e in range(2):
                        kt = 2 * kp + e
                        cols_ = slice(e * 512, (e + 1) * 512)
                        mm = mm3(dst, l_hi[:, kt, :], l_lo[:, kt, :], r_hi[:, cols_], r_lo[:, cols_],
                                 kt == 0, kt == KT - 1)
                    if kp == 3:
                        mm.then_inc(main_done, 1)
                    elif last_tile:
                        mm.then_inc(used, 1)
                    if kp == 1 and middle is not None:
                        middle()

            def channel_major(kind, n, half, dst, done):
                c = (kind, n)
                l_hi, l_lo = chunk(c)
                toks = slice(half * 512, (half + 1) * 512)
                for kt in range(KT):
                    w = slice(kt * P, (kt + 1) * P)
                    mm = mm3(dst, l_hi[:, w], l_lo[:, w], hT_hi[:, kt, toks], hT_lo[:, kt, toks],
                             kt == 0, kt == KT - 1)
                mm.then_inc(done, 1)

            def transposes(key, srcs):
                side_wait(pe, key)
                b = side_bank(key)
                for q, src in enumerate(srcs):
                    tr = nc.tensor.transpose(ps[:, b, q * P:(q + 1) * P], src, ident[:])
                tr.then_inc(side_done, 1)

            def x_transposes(s):
                pe.wait_ge(xhat, s + 1)
                for half in range(2):
                    transposes(("x", s, half), [x_tile(s)[:, (4 * half + q) * P:(4 * half + q + 1) * P]
                                                for q in range(4)])

            def main(key, middle=None):
                i = MIDX[key]
                kind, t = key
                main_wait(pe, i)
                l_hi, l_lo, s = h_tile(t)
                pe.wait_ge(h_ready, s + 1)
                last = {"k": TILES, "v": VTILES, "q": range(NT), "g": range(NT)}[kind][-1]
                token_major(t == last, kind, ps[:, i % 2, :], l_hi, l_lo, middle)

            pe.wait_ge(first_in, 16 * 4)
            pe.wait_ge(silu_done, 1)
            for kt in range(KT):
                pe.wait_ge(ada_landed[kt], 16)
                for q in range(4):
                    mm = M(ps[0:2, 4 + q, :], lhsT=silu_c[:, kt, :], rhs=ada_in[:, kt, q * 512:(q + 1) * 512],
                           start=(kt == 0), stop=(kt == KT - 1))
            mm.then_inc(ada_done, 1)
            x_transposes(0)
            pe.wait_ge(rows_done, 4)
            for c in range(2 * KT):
                tr = nc.tensor.transpose(ps[:, 0, 2 * c:2 * c + 2], mod_rows[:, c * P:(c + 1) * P], ident[0:2, 0:2])
            tr.then_inc(modT_done, 1)

            def k_transposes(t):
                pe.wait_ge(roped, t + 1)
                transposes(("kt", t), [kv[:, t, q * P:(q + 1) * P] for q in range(4)])

            x_transposes(1)
            pe.wait_ge(mod_ready, 2)
            for s in range(10):
                main(("k", TILES[s]))
                if s >= 3:
                    k_transposes(s - 3)
                if s + 2 < 10:
                    x_transposes(s + 2)

            def kv_product(t):
                key = ("kv", t)
                side_wait(pe, key)
                pe.wait_ge(vcat_ready, 2 + 2 * (NT - t))
                for h in range(HEADS):
                    lo_p, a = HD * (h % 2), h // 2
                    mm = M(ps[lo_p:lo_p + HD, side_bank(key), a * P:(a + 1) * P],
                           lhsT=kv[:, t, h * HD:(h + 1) * HD],
                           rhs=vcat[:, (NT - 1 - t) % 2, h * P:(h + 1) * P], start=True, stop=True)
                mm.then_inc(side_done, 1)

            for j, t in enumerate(VTILES):
                main(("v", t))
                if j == 0:
                    k_transposes(7)
                if j == 2:
                    pe.wait_ge(vcat_ready, 2)
                    for r in range(2):
                        i = MIDX[("v", VTILES[r])]
                        pe.wait_ge(main_free[i % 2], i // 2 + 1)
                        i = MIDX[("k", TILES[r])]
                        pe.wait_ge(main_free[i % 2], i // 2 + 1)
                    for h in range(HEADS):
                        lo_p, a = HD * (h % 2), h // 2
                        for r in range(2):
                            mm = M(ps[lo_p:lo_p + HD, 7, a * P:(a + 1) * P],
                                   lhsT=k_c[:, r, h * HD:(h + 1) * HD],
                                   rhs=vcat_c[:, r, h * P:(h + 1) * P], start=(r == 0), stop=(r == 1))
                    mm.then_inc(kvc_done, 1)
                if j >= 3:
                    kv_product(VTILES[j - 1])

            def head_rows(x, h, cols_):
                return x[HD * (h % 2):HD * (h % 2) + HD, h // 2, cols_]

            def scores(n):
                toks = slice(n * P, (n + 1) * P)
                if n:
                    pe.wait_ge(combined, n)
                side_out(pe, ("qt", n))
                side_out(pe, ("kt", n))
                for h in range(HEADS):
                    mm = M(ps[:, 4 + h % 2, (h // 2) * P:(h // 2 + 1) * P],
                           lhsT=head_rows(kT, h, toks), rhs=head_rows(qT, h, toks), start=True, stop=True)
                mm.then_inc(scores_done, 1)

            def inter(n):
                if n:
                    pe.wait_ge(combined, n)
                side_out(pe, ("qt", n))
                pe.wait_ge(states_ready, n + 1)
                toks = slice(n * P, (n + 1) * P)
                for h in range(HEADS):
                    a = h // 2
                    mm = M(ps[:, 6 + h % 2, a * P:(a + 1) * P], lhsT=head_rows(qT, h, toks),
                           rhs=kv[HD * (h % 2):HD * (h % 2) + HD, n, a * P:(a + 1) * P], start=True, stop=True)
                mm.then_inc(inter_done, 1)

            def intra(n):
                pe.wait_ge(masked, 2 * (n + 1))
                for h in range(HEADS):
                    a = h // 2
                    mm = M(ps[:, 4 + h % 2, a * P:(a + 1) * P], lhsT=aT[:, h, :],
                           rhs=v[:, n, a * P:(a + 1) * P], start=True, stop=True)
                mm.then_inc(intra_done, 1)

            for j in range(18):
                middle = (lambda n=j - 3: intra(n)) if 3 <= j <= 10 else None
                if j < 2 * NT:
                    main(("q", j) if j < NT else ("g", j - NT), middle)
                elif j == 16:
                    main_wait(pe, MIDX[("u", 0, 0)])
                    channel_major("u", 0, 0, ps[:, 0, :], main_done)
                if j == 0:
                    kv_product(0)
                if 1 <= j <= 8:
                    t = j - 1
                    pe.wait_ge(roped, NT + t + 1)
                    transposes(("qt", t), [qa[:, q * P:(q + 1) * P] for q in range(4)])
                if 2 <= j <= 9:
                    inter(j - 2)
                    scores(j - 2)
                if 10 <= j <= 17:
                    n = j - 10
                    pe.wait_ge(r_ready, n + 1)
                    transposes(("rt", n), [v[:, n, q * P:(q + 1) * P] for q in range(4)])

            for g in range(GROUPS):
                for half in range(2):
                    if g + half:
                        main_wait(pe, MIDX[("u", g, half)])
                        channel_major("u", g, half, ps[:, half, :], main_done)

            pe.wait_ge(late_in, 48)
            pe.wait_ge(ue_ready, GROUPS)
            for nt in range(4):
                for part in range(2):
                    if nt >= 2:
                        pe.wait_ge(pq_free, 2 * (nt - 2) + part + 1)
                    src = (u_e, u_o)[part]
                    for g in range(GROUPS):
                        mm = M(ps[:, 4 + 2 * (nt % 2) + part, g * P:(g + 1) * P],
                               lhsT=src[:, g, nt * P:(nt + 1) * P], rhs=mcs[:, part, :], start=True, stop=True)
                    mm.then_inc(pq_done, 1)
                if nt == 0:
                    pe.wait_ge(uc_ready, 1)
                    side_out(pe, ("rt", 6))
                    side_out(pe, ("rt", 7))
                    for g in range(GROUPS):
                        M(ps[HD * (g % 2):HD * (g % 2) + HD, 3, 2 * (g // 2):2 * (g // 2) + 2],
                          lhsT=mcs[:, 0, 0:64], rhs=u_c[:, :, g], start=True, stop=True)
                    for r in range(2):
                        mm = M(ps[0:GROUPS, 3, 4 + 2 * r:6 + 2 * r], lhsT=u_c[:, r, :], rhs=mcs[:, 0, 64:66],
                               start=True, stop=True)
                    mm.then_inc(cols_done, 1)

            pe.wait_ge(main_free[1], MIDX[("u", 3, 1)] // 2 + 1)
            pe.wait_ge(main_free[0], MIDX[("u", 3, 0)] // 2 + 1)
            pe.wait_ge(cols_free, 1)
            for nt in range(4):
                pe.wait_ge(pq_free, 2 * nt + 2)
                r_hi, r_lo = chunk(("cs", nt))
                first, last = nt == 0, nt == 3
                for part in range(2):
                    l_hi, l_lo = ((pa_hi, pa_lo), (pb_hi, pb_lo))[part]
                    cs = slice(part * 512, (part + 1) * 512)
                    for p in range(2):
                        w = slice(p * P, (p + 1) * P)
                        mm3(ps[:, 2 * part + p, :], l_hi[:, nt, w], l_lo[:, nt, w], r_hi[:, cs], r_lo[:, cs],
                            first, last)
                if nt == 0:
                    pe.wait_ge(pq_free, 5)
                mm3(ps[0:GROUPS, 4, :], pn_hi[:, nt, :], pn_lo[:, nt, :], r_hi[:, 0:512], r_lo[:, 0:512],
                    first, last).then_inc(dft_done, 1)

            def reduce_row(a, bank):
                pe.wait_ge(ada_acc_done, 8 * (a + 1))
                for half in range(2):
                    M(ps[0:1, bank + half, :], lhsT=ones[:], rhs=ada_acc[:, half * 512:(half + 1) * 512],
                      start=True, stop=True).then_inc(ada_red, 1)

            for m in range(KT):
                for half in range(2):
                    if m:
                        if half == 0:
                            pe.wait_ge(col_free, m)
                    else:
                        pe.wait_ge(ab_ready, 1 + half)
                    channel_major("ga", m, half, ps[:, half, :], merge_done)
                if m in (2, 4, 6):
                    pe.wait_ge(ret_free, m)
                    reduce_row(m // 2 - 1, 6)
                for half in range(2):
                    if m:
                        pe.wait_ge(gates_done, 2 * m)
                    else:
                        pe.wait_ge(ab_ready, 3 + half)
                    channel_major("gb", m, half, ps[:, 2 + half, :], merge_done)
                w_hi, w_lo = chunk(("fr", m))
                ms_ = slice(m * P, (m + 1) * P)
                if m == 0:
                    pe.wait_ge(ab_ready, 6)
                else:
                    pe.wait_ge(four_free, m)
                for p in range(2):
                    w = slice(p * P, (p + 1) * P)
                    mm3(ps[:, 4, :], w_hi[:, w], w_lo[:, w], ab_hi[:, p, :], ab_lo[:, p, :], p == 0, False)
                mm3(ps[:, 4, :], wn_hi[:, ms_], wn_lo[:, ms_], an_hi[:], an_lo[:], False, True).then_inc(merge_done, 1)
                for p in range(2):
                    w = slice((2 + p) * P, (3 + p) * P)
                    mm = mm3(ps[:, 5, :], w_hi[:, w], w_lo[:, w], ab_hi[:, 2 + p, :], ab_lo[:, 2 + p, :],
                             p == 0, p == 1)
                mm.then_inc(merge_done, 1)
                pe.wait_ge(gates_done, 2 * m + 1)
                for p in range(2):
                    w = slice(p * P, (p + 1) * P)
                    mm3(ps[:, 0, 0:2], w_hi[:, w], w_lo[:, w], a5_hi[:, p, :], a5_lo[:, p, :], p == 0, False)
                mm3(ps[:, 0, 0:2], wn_hi[:, ms_], wn_lo[:, ms_], n5_hi[:], n5_lo[:], False, True
                    ).then_inc(merge_done, 1)
                if m in (2, 4, 6):
                    pe.wait_ge(ada_row_out, m)
                elif m:
                    pe.wait_ge(ret_free, m)
                for half in range(2):
                    toks = slice(half * 512, (half + 1) * 512)
                    for kt in range(4):
                        w = slice((4 + kt) * P, (5 + kt) * P)
                        mm = mm3(ps[:, 6 + half, :], w_hi[:, w], w_lo[:, w], rT_hi[:, kt, toks],
                                 rT_lo[:, kt, toks], kt == 0, kt == 3)
                    mm.then_inc(merge_done, 1)
            pe.wait_ge(gates_done, 2 * KT)
            reduce_row(3, 2)

            def z_transposes(t):
                pe.wait_ge(xhat, 10 + t + 1)
                for half in range(2):
                    transposes(("z", t, half), [(xh, xh_b)[t % 2][:, (4 * half + q) * P:(4 * half + q + 1) * P]
                                                for q in range(4)])

            pe.wait_ge(ret_free, KT)
            def out_step(nh, t, kp):
                i = nh * NT + t
                toks = slice(t * P, (t + 1) * P)
                r_hi, r_lo = chunk(("wo", 4 * nh + kp))
                if i == 0:
                    pe.wait_ge(split, INDEX[("y", min(2 * kp + 1, 6))] + 1)
                for e in range(2):
                    kt = 2 * kp + e
                    if i == 0 and kt == KT - 1:
                        pe.wait_ge(y7_ready, 1)
                    cs = slice(e * 512, (e + 1) * 512)
                    mm = mm3(ps[:, 4 + i % 4, :], yT_hi[:, kt, toks], yT_lo[:, kt, toks], r_hi[:, cs],
                             r_lo[:, cs], kt == 0, kt == KT - 1)
                if kp == 3:
                    mm.then_inc(o_done, 1)
                elif t == NT - 1:
                    mm.then_inc(used, 1)

            for kp in range(4):
                for t in range(4):
                    out_step(0, t, kp)
            for i in range(4, 2 * NT):
                nh, t = i // NT, i % NT
                pe.wait_ge(o_free, i - 3)
                for kp in range(4):
                    out_step(nh, t, kp)
                if nh and t >= 2:
                    z_transposes(t - 2)
            z_transposes(NT - 2)

            def up(f, b):
                half, c = f // FFB, f % FFB
                pe.wait_ge(ff_free, b * 8 + (f + 1))
                pe.wait_ge(split, b * 8 + (MLP0 + c + 1))
                l_hi, l_lo = w1_slot(c)
                toks = slice(half * 512, (half + 1) * 512)
                for kt in range(KT):
                    w = slice(kt * P, (kt + 1) * P)
                    mm = mm3(ps[:, f % 2, :], l_hi[:, w], l_lo[:, w], h2_hi[:, kt, toks], h2_lo[:, kt, toks],
                             kt == 0, kt == KT - 1)
                mm.then_inc(ff_done, 1)

            def down(i, b):
                t, nh = i // 2, i % 2
                pe.wait_ge(o_free, b * 16 + (16 + i - 3))
                for c in range(FFB):
                    if i == 0:
                        pe.wait_ge(split, b * 8 + (MLP0 + FFB + c + 1))
                        pe.wait_ge(ff_free, b * 8 + (2 + c + 1))
                    if i == 8:
                        pe.wait_ge(ff_free, b * 8 + (2 + FFB + c + 1))
                    r_hi, r_lo = w2_slot(c)
                    toks, cs = slice(t * P, (t + 1) * P), slice(nh * 512, (nh + 1) * 512)
                    mm = mm3(ps[:, 4 + i % 4, :], ff_hi[:, c, toks], ff_lo[:, c, toks], r_hi[:, cs], r_lo[:, cs],
                             c == 0, c == FFB - 1)
                mm.then_inc(o_done, 1)

            def downs(b):
                for i in range(16):
                    down(i, b)

            for f in range(8):
                if f % FFB == 0:
                    pe.wait_ge(h_ready, 14 + f)
                up(f, 0)
                if f == 0:
                    z_transposes(NT - 1)
            downs(0)
            with pe.Fori(1, BLOCKS) as b:
                for f in range(8):
                    up(f, b)
                downs(b)


def constants():
    i = np.arange(P, dtype=np.float64)
    posc = np.zeros((P, 5, 16))
    posc[:, 0, :8], posc[:, 0, 8:] = (i + 1)[:, None], (P - i)[:, None]
    posc[:, 1, :8], posc[:, 1, 8:] = (P - 1 - i)[:, None], i[:, None]
    for r in range(2):
        posc[:, 2 + r, :8], posc[:, 2 + r, 8:] = (CTX - 1 - r * P - i)[:, None], (r * P + i)[:, None]
    posc[:, 4, :] = P
    diff = i[None, :] - i[:, None]
    dist = np.stack([np.maximum(diff, 0), np.maximum(-diff, 0), (diff >= 0) * HD ** -0.5, (diff <= 0) * HD ** -0.5], 1)
    nf = HD // 4
    inv = np.float32(10000.0) ** (-np.arange(nf, dtype=np.float32) / np.float32(nf))
    tok = np.arange(SEQ)
    ang = np.concatenate([(tok // 64).astype(np.float32)[:, None] * inv, (tok % 64).astype(np.float32)[:, None] * inv],
                         -1).astype(np.float64)
    rope = np.stack([np.cos(ang), np.sin(ang)], 1).reshape(NT, P, 2, HD // 2).transpose(1, 0, 2, 3)
    c = np.arange(P)[:, None]
    mcs = np.zeros((P, 2, P))
    mcs[:, 0, :65] = np.cos(2 * np.pi * ((c * np.arange(65)) % P) / P) * P ** -0.5
    mcs[:, 1, :64] = np.sin(2 * np.pi * ((c * np.arange(64)) % P) / P) * P ** -0.5
    n = np.arange(HALF)
    ph = 2 * np.pi * ((n[:, None] * n[None, :]) % SEQ) / SEQ
    dft = np.concatenate([np.cos(ph), np.sin(ph)], 1).reshape(4, P, CW) * SEQ ** -0.5
    sgn = np.broadcast_to((1 - 2 * (n % 2)) * SEQ ** -0.5, (P, HALF))
    coef = np.ones((P, 4))
    coef[0, :2] = coef[64, :2] = 0
    coef[:, 2:] = -1
    out = {"posc": posc, "dist": dist, "rope": rope, "mcs": mcs, "dft": dft, "sgn": sgn, "coef": coef,
           "ident": np.eye(P)}
    return {k: np.ascontiguousarray(a, dtype=np.float32) for k, a in out.items()}


def layouts(a):
    w_in, w_out = a["w_in"][0], a["w_out"][0]

    def token_major(w, col):
        return w[:, col:col + 512].reshape(4, 2, P, 512).transpose(0, 2, 1, 3).reshape(4, P, CW)

    def channel_major(w, col):
        return w[:, col:col + P].reshape(KT, P, P).transpose(1, 0, 2).reshape(P, CW)

    part = {"k": 2 * RW, "v": 3 * RW, "q": RW, "g": 4 * RW, "u": 0, "ga": 5 * RW, "gb": 5 * RW + D}
    chunks = []
    for kind, i in STREAM:
        if kind in ("k", "v", "q", "g"):
            chunks.append(token_major(w_in, part[kind])[i])
        elif kind in ("u", "ga", "gb"):
            chunks.append(channel_major(w_in, part[kind] + i * P))
        elif kind == "wo":
            chunks.append(token_major(w_out, 512 * (i // 4))[i % 4])
    w4 = a["four_w_out"][0]
    rows, partners = [], []
    for tile in range(4):
        for g in (2 * (tile % 2), 2 * (tile % 2) + 1):
            for d in range(64):
                rows.append(g * P + d)
                partners.append(g * P + (P - d) % P)

    def by_tile(idx):
        return w4[np.array(idx)].reshape(4, P, KT, P).transpose(2, 1, 0, 3)

    col = lambda v: np.ascontiguousarray(v.reshape(-1, P).T)
    b_ada = a["b_ada"]
    return {
        "x": a["x"][0], "ctx": a["ctx"][0],
        "cc": np.stack([a["c"][0], a["c_ctx"]], -1).reshape(KT, P, 2).transpose(1, 0, 2),
        "w_ada": a["w_ada"][0], "b_ada": b_ada,
        "b_rows": np.concatenate([b_ada[:, :2 * D], b_ada[:, :2 * D]], 0),
        "bmod2": b_ada[0, 3 * D:5 * D].reshape(2, KT, P).transpose(2, 0, 1),
        "gain1": col(a["norm1_gain"][0]), "gain2": col(a["norm2_gain"][0]),
        "logits": np.broadcast_to(a["ret_decay_logit"][0].reshape(1, 16), (P, 16)),
        "gn_rows": np.broadcast_to(a["ret_gn_gain"], (P, RW)),
        "final_gain": a["final_gain"][None, :],
        "w_stream": np.stack(chunks),
        "four_stream": np.stack([by_tile(rows), by_tile(partners)], 2).reshape(KT, P, 2, 512),
        "four_nyq": w4[64::P],
        "ret_stream": a["ret_w_out"][0].reshape(4, P, KT, P).transpose(2, 1, 0, 3).reshape(KT, P, 512),
        "w1_stream": a["w_mlp1"][0].reshape(KT, P, DFF // P, P).transpose(2, 1, 0, 3).reshape(DFF // P, P, CW),
        "w2_stream": a["w_mlp2"][0].reshape(DFF // P, P, D),
    }


def build(nc, shapes):
    ins = {k: nc.dram_tensor(f"in_{k}", s, F32, kind="ExternalInput").ap() for k, s in shapes.items()}
    out = nc.dram_tensor("out", (SEQ, D), F32, kind="ExternalOutput").ap()
    program(nc, ins, out)


def kernel(**inputs):
    import concourse.bacc as bacc
    from concourse.bass_utils import run_bass_kernel_spmd

    arrays = layouts({k: np.asarray(v) for k, v in inputs.items()})
    arrays.update(constants())
    arrays = {k: np.ascontiguousarray(v) for k, v in arrays.items()}
    nc = bacc.Bacc("TRN2", target_bir_lowering=False, num_devices=1)
    build(nc, {k: v.shape for k, v in arrays.items()})
    r = run_bass_kernel_spmd(nc, [{f"in_{k}": v for k, v in arrays.items()}], core_ids=[0])
    return r.results[0]["out"].reshape(1, SEQ, D)
```

```python
from contextlib import ExitStack

import concourse.bass as bass
from concourse import mybir
import numpy as np

F32 = mybir.dt.float32
F32R = mybir.dt.float32r
ALU = mybir.AluOpType
ACT = mybir.ActivationFunctionType
AX = mybir.AxisListType

P = 128
D = 1024
SEQ = 1024
CTX = 256
DFF = 4 * D
KT = D // P
NT = SEQ // P
NC_ = CTX // P
HEADS = 8
HD = 64
PAIRS = HEADS // 2
RW = HEADS * HD
GROUPS = 4
HALF = SEQ // 2
EPS = 1e-6
RING = 6
CW = 1024
FFB = 4
BLOCKS = DFF // P // FFB

STREAM = ([("k", i) for i in range(4)] + [("v", i) for i in range(4)] + [("q", i) for i in range(4)]
          + [("g", i) for i in range(4)] + [("u", i) for i in range(4)] + [("cs", i) for i in range(4)]
          + [(kind, m) for m in range(KT) for kind in ("ga", "gb", "fr")])
STREAM += [("wo", _i) for _i in range(8)]
INDEX = {c: i for i, c in enumerate(STREAM)}
RELEASED_EARLY = [c for c in STREAM if c[0] in ("k", "v", "q", "g", "wo") and c[1] % 4 < 3]
MLP0 = len(STREAM)
W_KINDS = ("k", "v", "q", "g", "u", "ga", "gb", "wo")
WIDX = {c: i for i, c in enumerate(c for c in STREAM if c[0] in W_KINDS)}

TILES = ["c0", "c1"] + list(range(NT))
VTILES = ["c0", "c1"] + list(range(NT - 1, -1, -1))
MAIN = ([("k", t) for t in TILES] + [("v", t) for t in VTILES] + [("q", t) for t in range(NT)]
        + [("g", t) for t in range(NT)] + [("u", g, h) for g in range(GROUPS) for h in range(2)])
MIDX = {c: i for i, c in enumerate(MAIN)}
SIDE = [("x", 0, 0), ("x", 0, 1), ("x", 1, 0), ("x", 1, 1)]
for _s in range(10):
    if _s >= 3:
        SIDE += [("kt", _s - 3)]
    if _s + 2 < 10:
        SIDE += [("x", _s + 2, 0), ("x", _s + 2, 1)]
SIDE += [("kt", 7)] + [("kv", t) for t in range(7, 0, -1)] + [("kv", 0)]
for _j in range(1, 18):
    if _j - 1 < 8:
        SIDE += [("qt", _j - 1)]
    if 10 <= _j <= 17:
        SIDE += [("rt", _j - 10)]
SIDE += [("z", t, h) for t in range(NT) for h in range(2)]
SIDX = {c: i for i, c in enumerate(SIDE)}


def program(nc, ins, out):
    with ExitStack() as ctx:
        def sem(name):
            return ctx.enter_context(nc.semaphore(name))

        arena = ctx.enter_context(nc.sbuf_tensor("arena", [P, 53200], F32))
        base = 16512
        at = {}

        def place(name, off, shape, dt=F32):
            size = int(np.prod(shape[1:])) * 4
            assert base + off + size <= 229344, (name, off, size)
            at[name] = nc.alloc_sbuf_tensor_at(name, shape, dt, offset=base + off)
            return at[name]

        ring_hi = place("ring_hi", 0, [P, RING, CW], F32R)
        ring_lo = place("ring_lo", 24576, [P, RING, CW], F32R)
        raw = place("raw", 49152, [P, 2, CW])
        o_ht = 57344
        ada_in = place("ada_in", o_ht, [P, KT, 2 * D])
        hT_hi = place("hT_hi", o_ht, [P, KT, SEQ], F32R)
        hT_lo = place("hT_lo", o_ht + 32768, [P, KT, SEQ], F32R)
        yT_hi = place("yT_hi", o_ht, [P, KT, SEQ], F32R)
        yT_lo = place("yT_lo", o_ht + 32768, [P, KT, SEQ], F32R)
        y_in = place("y_in", o_ht + 32768, [P, KT, SEQ])
        h2_hi = place("h2_hi", o_ht, [P, KT, SEQ], F32R)
        h2_lo = place("h2_lo", o_ht + 32768, [P, KT, SEQ], F32R)
        o_kt = o_ht + 65536
        o_qt, o_kv, o_v = o_kt + 16384, o_kt + 32768, o_kt + 49152
        o_m = o_kt + 65536
        x_a = place("x_a", o_kt, [P, 3, D])
        x_b = place("x_b", o_v, [P, 4, D])
        ctx_in = place("ctx_in", o_kv, [P, 2, D])
        mod_rows = place("mod_rows", o_kv + 8192, [2, 2 * D])
        hc_hi = place("hc_hi", o_qt, [P, KT, CTX], F32R)
        hc_lo = place("hc_lo", o_qt + 8192, [P, KT, CTX], F32R)
        kT = place("kT", o_kt, [P, PAIRS, SEQ])
        qT = place("qT", o_qt, [P, PAIRS, SEQ])
        kv = place("kv", o_kv, [P, NT, RW])
        v = place("v", o_v, [P, NT, RW])
        vcat_c = place("vcat_c", o_v, [P, 2, 2 * RW])
        rT_hi = place("rT_hi", o_kt, [P, PAIRS, SEQ], F32R)
        rT_lo = place("rT_lo", o_qt, [P, PAIRS, SEQ], F32R)
        u_e = place("u_e", o_v, [P, GROUPS, HALF])
        u_o = place("u_o", o_v + 8192, [P, GROUPS, HALF])
        fj = place("fj", o_kv, [P, HALF])
        pa_hi = place("pa_hi", o_kv, [P, 4, 256], F32R)
        pa_lo = place("pa_lo", o_kv + 4096, [P, 4, 256], F32R)
        pb_hi = place("pb_hi", o_kv + 8192, [P, 4, 256], F32R)
        pb_lo = place("pb_lo", o_kv + 12288, [P, 4, 256], F32R)
        ab_hi = place("ab_hi", o_v, [P, 4, HALF], F32R)
        ab_lo = place("ab_lo", o_v + 8192, [P, 4, HALF], F32R)
        y = place("y", o_kv, [P, SEQ])
        sig_a = place("sig_a", o_kv + 4096, [P, SEQ])
        sig_b = place("sig_b", o_kv + 8192, [P, SEQ])
        ada_raw = place("ada_raw", o_kv + 12288, [P, D])
        wn_raw = place("wn_raw", o_kv, [GROUPS, D])
        acc = place("acc", o_kt, [P, NT, D])
        g1b = place("g1b", o_kv, [P, D])
        b1b = place("b1b", o_kv + 4096, [P, D])
        b2b = place("b2b", o_kv + 8192, [P, D])
        xh = place("xh", o_kv + 12288, [P, D])
        h2_f = place("h2_f", o_kv + 16384, [P, D])
        xh_b = place("xh_b", o_kv + 28672, [P, D])
        gated = place("gated", o_kv + 20480, [P, 512])
        h2_g = place("h2_g", o_kv + 24576, [P, D])
        ff_hi = place("ff_hi", o_kv, [P, FFB, SEQ], F32R)
        ff_lo = place("ff_lo", o_kv + 16384, [P, FFB, SEQ], F32R)
        pos = [o_m]

        def small(name, shape, dt=F32):
            t = place(name, pos[0], shape, dt)
            pos[0] += (int(np.prod(shape[1:])) * 4 + 31) // 32 * 32
            return t

        ident = small("ident", [P, P])
        cc = small("cc", [P, KT, 2])
        silu_c = small("silu_c", [P, KT, 2])
        gain1 = small("gain1", [P, KT])
        gain2 = small("gain2", [P, KT])
        mod = small("mod", [P, 2 * KT, 2])
        a1 = small("a1", [P, KT, 2])
        mod2 = small("mod2", [P, 2, KT])
        bmod2 = small("bmod2", [P, 2, KT])
        a2 = small("a2", [P, KT])
        ss = small("ss", [P, 16])
        ms = small("ms", [P, 16])
        rt = small("rt", [P, 16])
        rstd = small("rstd", [P, 16])
        lgt = small("lgt", [P, 16])
        lw = small("lw", [P, 6, 16])
        lg = small("lg", [P, 16])
        posc = small("posc", [P, 5, 16])
        dec = small("dec", [P, 5, 16])
        dec_s = small("dec_s", [P, PAIRS, 2])
        coef = small("coef", [P, 4])
        hss = small("hss", [P, 8, 4])
        u_c = small("u_c", [P, 2, GROUPS])
        cols = small("cols", [P, 2, 2])
        cols_n = small("cols_n", [GROUPS, 4])
        a5_hi = small("a5_hi", [P, 2, 2], F32R)
        a5_lo = small("a5_lo", [P, 2, 2], F32R)
        n5_hi = small("n5_hi", [GROUPS, 2], F32R)
        n5_lo = small("n5_lo", [GROUPS, 2], F32R)
        pn_hi = small("pn_hi", [P, 4, GROUPS], F32R)
        pn_lo = small("pn_lo", [P, 4, GROUPS], F32R)
        ones = small("ones", [P, 1])
        o_t = pos[0]
        dmask = place("dmask", o_t, [P, HEADS, P])
        rope = place("rope", o_t + 4096, [P, NT, 2, HD // 2])
        h_f = place("h_f", o_t + 6144, [P, D])
        wp_v = place("wp_v", o_t + 6144, [P, 2, 512])
        wp_g = place("wp_g", o_t + 10240, [P, 2, 512])
        aT = place("aT", o_t + 6144, [P, HEADS, P])
        t1 = place("t1", o_t + 10240, [P, 2, RW])
        dist = place("dist", o_t + 10240, [P, 4, P])
        dtmp = place("dtmp", o_t + 12288, [P, 2, 3, P])
        k_c = place("k_c", o_t + 15360, [P, 2, RW])
        junk = place("junk", o_t + 16384, [P, D])
        vcat = place("vcat", o_t + 10240, [P, 2, 2 * RW])
        it = place("it", o_t + 10240, [P, 4, 2, HD])
        st_f = place("st_f", o_t + 12288, [P, 2, PAIRS, HD])
        sq = place("sq", o_t + 14336, [P, RW])
        qb = place("qb", o_t + 16384, [P, RW])
        qa = place("qa", o_t + 18432, [P, RW])
        st_b = place("st_b", o_t + 18432, [P, 2, PAIRS, HD])
        gnb = place("gnb", o_t + 4096, [P, RW])
        sg = place("sg", o_t + 16384, [P, 2, RW])
        mcs = place("mcs", o_t, [P, 2, P])
        u_lo = place("u_lo", o_t + 3072, [P, HALF])
        sgn = place("sgn", o_t + 1024, [P, HALF])
        ft = place("ft", o_t + 5120, [P, HALF])
        an_hi = place("an_hi", o_t + 8192, [GROUPS, HALF], F32R)
        an_lo = place("an_lo", o_t + 10240, [GROUPS, HALF], F32R)
        wn_hi = place("wn_hi", o_t + 12288, [GROUPS, D], F32R)
        wn_lo = place("wn_lo", o_t + 16384, [GROUPS, D], F32R)
        b_sb = place("b_sb", o_t, [P, HALF])
        ada_acc = place("ada_acc", o_t + 2048, [P, D])
        ada_row = place("ada_row", o_t + 6144, [1, 512])
        x_hi = place("x_hi", o_t, [P, 2, CW], F32R)
        x_lo = place("x_lo", o_t + 8192, [P, 2, CW], F32R)
        g2b = place("g2b", o_t + 16384, [P, D])
        fgb = place("fgb", o_t, [P, D])
        o_sb = place("o_sb", o_t + 4096, [P, 2, D])
        junk3 = place("junk3", o_t + 12288, [P, D])

        ps = ctx.enter_context(nc.psum_tensor("ps", [P, 8, 512], F32))

        y_scr = nc.dram_tensor("y_scr", [KT, P, SEQ], F32, kind="Internal").ap()
        wpm_scr = nc.dram_tensor("wpm_scr", [KT, P, 512], F32, kind="Internal").ap()
        mod_scr = nc.dram_tensor("mod_scr", [4, D], F32, kind="Internal").ap()

        raw_in = [sem("raw_in0"), sem("raw_in1")]
        hi_done = sem("hi_done")
        split = sem("split")
        used = sem("used")
        c_in = sem("c_in")
        first_in = sem("first_in")
        decay_in = sem("decay_in")
        params_in = sem("params_in")
        ada_landed = [sem(f"ada_landed{i}") for i in range(KT)]
        x_landed = [sem(f"x_landed{i}") for i in range(10)]
        late_in = sem("late_in")
        silu_done = sem("silu_done")
        ada_done = sem("ada_done")
        rows_done = sem("rows_done")
        modT_done = sem("modT_done")
        mod_ready = sem("mod_ready")
        dve_step = sem("dve_step")
        pool_step = sem("pool_step")
        sumsq = sem("sumsq")
        meansq = sem("meansq")
        root = sem("root")
        rstd_ready = sem("rstd_ready")
        xhat = sem("xhat")
        hhi_done = sem("hhi_done")
        h_ready = sem("h_ready")
        main_done = sem("main_done")
        main_free = [sem("main_free0"), sem("main_free1")]
        side_done = sem("side_done")
        side_free = [sem("side_free0"), sem("side_free1")]
        decay_log = sem("decay_log")
        decay_exp = sem("decay_exp")
        roped = sem("roped")
        vcat_ready = sem("vcat_ready")
        states_ready = sem("states_ready")
        kvc_done = sem("kvc_done")
        scores_done = sem("scores_done")
        masked = sem("masked")
        intra_done = sem("intra_done")
        inter_done = sem("inter_done")
        combined = sem("combined")
        o_ready = sem("o_ready")
        r_ready = sem("r_ready")
        wp_in = sem("wp_in")
        wpm_stored = sem("wpm_stored")
        ue_ready = sem("ue_ready")
        uc_ready = sem("uc_ready")
        cols_done = sem("cols_done")
        cols_free = sem("cols_free")
        pq_done = sem("pq_done")
        pq_free = sem("pq_free")
        dft_done = sem("dft_done")
        ab_ready = sem("ab_ready")
        wn_in = sem("wn_in")
        merge_done = sem("merge_done")
        gates_done = sem("gates_done")
        four_free = sem("four_free")
        col_free = sem("col_free")
        ret_free = sem("ret_free")
        y_ready = sem("y_ready")
        y_stored = sem("y_stored")
        y_landed = [sem(f"y_landed{i}") for i in range(KT - 1)]
        y_hi_done = sem("y_hi_done")
        y_split = sem("y_split")
        y7_ready = sem("y7_ready")
        ada_raw_in = sem("ada_raw_in")
        ada_acc_done = sem("ada_acc_done")
        ada_red = sem("ada_red")
        ada_row_out = sem("ada_row_out")
        row_stored = sem("row_stored")
        acc_in = [sem(f"acc_in{i}") for i in range(4)]
        gate1_in = sem("gate1_in")
        gates_in = sem("gates_in")
        g_ready = sem("g_ready")
        o_done = sem("o_done")
        o_free = sem("o_free")
        x2_done = sem("x2_done")
        w2_scaled = sem("w2_scaled")
        ff_done = sem("ff_done")
        ff_relu = sem("ff_relu")
        ff_sq = sem("ff_sq")
        ff_hi_done = sem("ff_hi_done")
        ff_free = sem("ff_free")
        fin_in = sem("fin_in")
        y_out = sem("y_out")
        out_stored = [sem("out_stored0"), sem("out_stored1")]

        def released(c):
            kind, i = c
            if c in RELEASED_EARLY:
                return used, RELEASED_EARLY.index(c) + 1
            if kind in ("k", "v", "q", "g"):
                last = {"k": TILES, "v": VTILES, "q": range(NT), "g": range(NT)}[kind][-1]
                return main_done, MIDX[(kind, last)] + 1
            if kind == "u":
                return main_done, MIDX[("u", i, 1)] + 1
            if kind == "cs":
                return dft_done, i + 1
            if kind in ("ga", "gb", "fr"):
                return merge_done, 9 * i + {"ga": 2, "gb": 4, "fr": 9}[kind]
            return o_done, 8 * (i // 4 + 1)

        def slot(c):
            s = INDEX[c] % RING
            return ring_hi[:, s, :], ring_lo[:, s, :]

        def w1_slot(c):
            return (ring_hi[:, 2 + c, :], ring_lo[:, 2 + c, :]) if c < 2 else (x_hi[:, c - 2, :], x_lo[:, c - 2, :])

        def w2_slot(c):
            s = (0, 1, 4, 5)[c]
            return ring_hi[:, s, :], ring_lo[:, s, :]

        def main_wait(eng, i):
            if i >= 2:
                eng.wait_ge(main_free[i % 2], i // 2)

        def side_wait(eng, key):
            j = SIDX[key]
            if j >= 2:
                eng.wait_ge(side_free[j % 2], j // 2)

        def side_out(eng, key):
            j = SIDX[key]
            eng.wait_ge(side_free[j % 2], j // 2 + 1)

        def side_bank(key):
            return 2 + SIDX[key] % 2

        def h_tile(t):
            s = TILES.index(t)
            if s < 2:
                return hc_hi[:, :, s * P:(s + 1) * P], hc_lo[:, :, s * P:(s + 1) * P], s
            return hT_hi[:, :, t * P:(t + 1) * P], hT_lo[:, :, t * P:(t + 1) * P], s

        def x_tile(s):
            if s == 5:
                return ctx_in[:, 1, :]
            return ctx_in[:, s, :] if s < 2 else x_a[:, s - 2, :] if s < 5 else x_b[:, s - 6, :]

        class Steps:

            def __init__(self, eng, step):
                self.eng, self.step, self.count = eng, step, {}

            def __call__(self, ins, s=None):
                s = self.step if s is None else s
                ins.then_inc(s, 1)
                self.count[id(s)] = self.count.get(id(s), 0) + 1
                return self.count[id(s)]

            def chain(self, ins, s=None, value=None):
                n = self(ins, s)
                self.eng.wait_ge(self.step if s is None else s, n if value is None else value)

        def load_x(eng, s):
            src = ins["ctx"][s * P:(s + 1) * P, :] if s < 2 else ins["x"][(s - 2) * P:(s - 1) * P, :]
            eng.dma_start(x_tile(s), src).then_inc(x_landed[s], 16)

        block = ctx.enter_context(nc.Block())

        @block.sync
        def _(sp):
            for i, (kind, n) in enumerate(STREAM):
                if i < 3:
                    for kt in ((0,), (1,), range(2, KT))[i]:
                        sp.dma_start(ada_in[:, kt, :], ins["w_ada"][kt * P:(kt + 1) * P, 0:2 * D]
                                     ).then_inc(ada_landed[kt], 16)
                if i == 4:
                    load_x(sp, 2)
                    load_x(sp, 3)
                    for dst, name in ((gain2, "gain2"), (coef, "coef"), (bmod2, "bmod2"), (rope, "rope")):
                        sp.dma_start(dst[:], ins[name]).then_inc(params_in, 16)
                    for s in (4, 6, 7, 8, 9):
                        load_x(sp, s)
                if i >= 2:
                    sp.wait_ge(split, i - 1)
                dst = raw[:, i % 2, :]
                if kind in W_KINDS:
                    sp.dma_start(dst, ins["w_stream"][WIDX[(kind, n)]]).then_inc(raw_in[i % 2], 16)
                elif kind == "cs":
                    sp.dma_start(dst, ins["dft"][n]).then_inc(raw_in[i % 2], 16)
                else:
                    sp.wait_ge(wpm_stored, 16 * KT)
                    sp.dma_start(dst[:, 0:512], wpm_scr[n]).then_inc(raw_in[i % 2], 16)
                    sp.dma_start(dst[:, 512:1024], ins["ret_stream"][n]).then_inc(raw_in[i % 2], 16)
                if (kind, n) == ("wo", 3):
                    sp.wait_ge(merge_done, 9 * (KT - 1) + 4)
                    for t in range(KT - 1):
                        sp.wait_ge(y_stored, 16 * (t + 1))
                        sp.dma_start(y_in[:, t, :], y_scr[t]).then_inc(y_landed[t], 16)
            for c in range(FFB):
                i = MLP0 + c
                sp.wait_ge(split, i - 1)
                sp.dma_start(raw[:, i % 2, :], ins["w1_stream"][c]).then_inc(raw_in[i % 2], 16)

            def load_w2(b):
                for c in range(FFB):
                    i = MLP0 + FFB + c
                    sp.wait_ge(split, b * 8 + (i - 1))
                    sp.dma_start(raw[:, i % 2, :], ins["w2_stream"][b * FFB + c]).then_inc(raw_in[i % 2], 16)

            def load_next_w1(b):
                for c in range(FFB):
                    i = MLP0 + 8 + c
                    sp.wait_ge(split, b * 8 + (i - 1))
                    sp.dma_start(raw[:, i % 2, :], ins["w1_stream"][b * FFB + (FFB + c)]).then_inc(raw_in[i % 2], 16)

            with sp.Fori(0, BLOCKS - 1) as b:
                load_w2(b)
                load_next_w1(b)
            load_w2(BLOCKS - 1)
            for t in range(NT):
                sp.wait_ge(y_out, t + 1)
                sp.dma_start(out[t * P:(t + 1) * P, :], o_sb[:, t % 2, :]).then_inc(out_stored[t % 2], 16)
            for n in range(2):
                sp.wait_ge(out_stored[n], 16 * NT // 2)

        raw_seen = []
        landed = [0, 0]
        for i, (kind, n) in enumerate(STREAM):
            landed[i % 2] += 32 if kind == "fr" else 16
            raw_seen.append(landed[i % 2])
        raw_mlp = list(landed)

        def raw_wait(eng, i):
            eng.wait_ge(raw_in[i % 2], raw_seen[i])

        def raw_wait_mlp(eng, c, b):
            i = MLP0 + c
            k = c // 2 + 1
            eng.wait_ge(raw_in[i % 2], b * 64 + (raw_mlp[i % 2] + 16 * k))

        @block.gpsimd
        def _(pool):
            do = Steps(pool, pool_step)

            def lo(i):
                hi_ap, lo_ap = slot(STREAM[i])
                pool.wait_ge(hi_done, i + 1)
                nc.gpsimd.tensor_tensor(lo_ap, raw[:, i % 2, :], hi_ap.bitcast(F32),
                                        ALU.subtract).then_inc(split, 1)

            def w_plus_minus(m, wp):
                if m:
                    pool.wait_ge(wpm_stored, 16 * m)
                pool.dma_start(wp[:], ins["four_stream"][m]).then_inc(wp_in, 16)
                pool.wait_ge(wp_in, 16 * (m + 1))
                part = wp[:, 1, :].rearrange("p (t c) -> p t c", t=4)
                do.chain(nc.gpsimd.tensor_tensor(part, part, coef[:, :, None].to_broadcast([P, 4, P]), ALU.mult))
                do.chain(nc.gpsimd.tensor_tensor(wp[:, 0, :], wp[:, 0, :], wp[:, 1, :], ALU.add))
                pool.dma_start(wpm_scr[m], wp[:, 0, :]).then_inc(wpm_stored, 16)

            for i in range(4):
                lo(i)
            for n in range(10):
                if n == 2:
                    lo(4)
                    lo(5)
                hi_ap, lo_ap, _ = h_tile(TILES[n])
                pool.wait_ge(hhi_done, n + 1)
                for half in range(2):
                    side_out(pool, ("x", n, half))
                nc.gpsimd.tensor_tensor(lo_ap, h_f[:].rearrange("p (c t) -> p c t", c=KT), hi_ap.bitcast(F32),
                                        ALU.subtract).then_inc(h_ready, 1)
            for i in range(RING, INDEX[("q", 2)]):
                lo(i)
            pool.wait_ge(params_in, 16 * 4)
            pool.wait_ge(h_ready, 10)
            for m in range(4):
                w_plus_minus(m, wp_v)
            for i in range(INDEX[("q", 2)], INDEX[("u", 2)]):
                lo(i)
            pool.wait_ge(o_ready, NT)
            for m in range(4, 7):
                w_plus_minus(m, wp_g)
            for i in range(INDEX[("u", 2)], INDEX[("cs", 2)]):
                lo(i)
            w_plus_minus(7, wp_g)
            for i in range(INDEX[("cs", 2)], INDEX[("wo", 4)]):
                lo(i)
            for t in range(KT - 1):
                pool.wait_ge(y_hi_done, t + 1)
                nc.gpsimd.tensor_tensor(yT_lo[:, t, :], y_in[:, t, :], yT_hi[:, t, :].bitcast(F32),
                                        ALU.subtract).then_inc(y_split, 1)
            for i in range(INDEX[("wo", 4)], len(STREAM)):
                lo(i)

            def lo_mlp(c, b, hi_ap, lo_ap):
                i = MLP0 + c
                pool.wait_ge(hi_done, b * 8 + (i + 1))
                nc.gpsimd.tensor_tensor(lo_ap, raw[:, i % 2, :], hi_ap.bitcast(F32),
                                        ALU.subtract).then_inc(split, 1)

            def scale_w2(c, b):
                i = MLP0 + FFB + c
                raw_wait_mlp(pool, FFB + c, b)
                nc.gpsimd.tensor_tensor(raw[:, i % 2, :], raw[:, i % 2, :], g2b[:], ALU.mult).then_inc(w2_scaled, 1)

            for c in range(FFB):
                lo_mlp(c, 0, *w1_slot(c))
            def h2_lo_half(t):
                pool.wait_ge(hhi_done, 10 + t + 1)
                for half in range(2):
                    side_out(pool, ("z", t, half))
                nc.gpsimd.tensor_tensor(h2_lo[:, :, t * P:(t + 1) * P],
                                        (h2_f, h2_g)[t % 2][:].rearrange("p (c t) -> p c t", c=KT),
                                        h2_hi[:, :, t * P:(t + 1) * P].bitcast(F32), ALU.subtract).then_inc(h_ready, 1)

            for t in range(NT - 1):
                h2_lo_half(t)
            pool.wait_ge(g_ready, 2)

            def two_w2(c, b):
                scale_w2(c, b)
                scale_w2(c + 1, b)
                for i in range(c, c + 2):
                    lo_mlp(FFB + i, b, *w2_slot(i))

            def next_w1(b):
                for c in range(FFB):
                    lo_mlp(8 + c, b, *w1_slot(c))

            scale_w2(0, 0)
            scale_w2(1, 0)
            h2_lo_half(NT - 1)
            for c in range(2):
                lo_mlp(FFB + c, 0, *w2_slot(c))
            two_w2(2, 0)
            next_w1(0)
            with pool.Fori(1, BLOCKS - 1) as b:
                two_w2(0, b)
                two_w2(2, b)
                next_w1(b)
            two_w2(0, BLOCKS - 1)
            two_w2(2, BLOCKS - 1)

        @block.scalar
        def _(act):
            A = nc.scalar.activation

            def load(names, semaphore):
                for dst, name in names:
                    act.dma_start(dst[:], ins[name]).then_inc(semaphore, 16)

            load(((cc, "cc"),), c_in)
            load(((ident, "ident"), (gain1, "gain1"), (mod_rows, "b_rows")), first_in)
            load_x(act, 0)
            act.wait_ge(c_in, 16)
            A(silu_c[:], cc[:], ACT.Silu).then_inc(silu_done, 1)
            load(((lgt, "logits"), (posc, "posc"), (dist, "dist")), decay_in)
            load_x(act, 1)

            nhi = [0]

            def hi_to(key):
                while nhi[0] <= INDEX[key]:
                    i = nhi[0]
                    c = STREAM[i]
                    if i >= RING:
                        act.wait_ge(*released(STREAM[i - RING]))
                    raw_wait(act, i)
                    A(slot(c)[0], raw[:, i % 2, :], ACT.Copy).then_inc(hi_done, 1)
                    nhi[0] += 1

            def copy_side(key, dst, src):
                act.wait_ge(side_done, SIDX[key] + 1)
                A(dst, src, ACT.Copy).then_inc(side_free[SIDX[key] % 2], 1)

            def square(s):
                act.wait_ge(x_landed[s], 16)
                if s == 2:
                    act.wait_ge(rows_done, 4)
                if s:
                    act.wait_ge(sumsq, s)
                dst = junk[:] if s < 2 else ps[:, 4:6, :].rearrange("p a b -> p (a b)")
                A(dst, x_tile(s), ACT.Square, accum_out=ss[:, s:s + 1]).then_inc(sumsq, 1)

            def norm(s):
                act.wait_ge(meansq, s + 1)
                A(rt[:, s:s + 1], ms[:, s:s + 1], ACT.Sqrt).then_inc(root, 1)
                act.wait_ge(rstd_ready, s + 1)
                A(x_tile(s), x_tile(s), ACT.Identity, scale=rstd[:, s:s + 1]).then_inc(xhat, 1)

            hi_to(("k", 1))
            square(0)
            norm(0)
            act.wait_ge(decay_log, 1)
            A(lw[:, 1, :], lw[:, 0, :], ACT.Exp).then_inc(decay_exp, 1)
            act.wait_ge(decay_log, 2)
            A(lw[:, 3, :], lw[:, 2, :], ACT.Ln).then_inc(decay_exp, 1)
            act.wait_ge(decay_log, 3)
            A(dec[:], dec[:], ACT.Exp).then_inc(decay_exp, 1)
            square(1)
            norm(1)
            def mask_exps(h):
                if h >= 2:
                    act.wait_ge(decay_log, 3 + h - 1)
                for r in range(2):
                    A(dtmp[:, h % 2, r, :], dist[:, r, :], ACT.Exp,
                      scale=lg[:, 8 * r + h:8 * r + h + 1]).then_inc(decay_exp, 1)

            for h in range(5):
                mask_exps(h)
            hi_to(("k", 3))
            for s in range(1, 13):
                if 2 <= s < 10:
                    square(s)
                if 1 <= s <= 10:
                    for half in range(2):
                        side_out(act, ("x", s - 1, half))
                    hi_ap, _, _ = h_tile(TILES[s - 1])
                    A(hi_ap, h_f[:].rearrange("p (c t) -> p c t", c=KT), ACT.Copy).then_inc(hhi_done, 1)
                if s == 2:
                    hi_to(("v", 1))
                if 2 <= s < 10:
                    norm(s)
                if s == 2:
                    act.wait_ge(side_done, SIDX[("x", 1, 1)] + 1)
                    load_x(act, 5)
                for h in {1: (5, 6), 2: (7,)}.get(s, ()):
                    mask_exps(h)
                if 2 <= s <= 3:
                    i = MIDX[("k", TILES[s - 2])]
                    act.wait_ge(main_done, i + 1)
                    A(k_c[:, s - 2, :], ps[:, i % 2, :], ACT.Copy).then_inc(main_free[i % 2], 1)
                if s == 12:
                    hi_to(("q", 1))
                if s >= 5:
                    t = s - 5
                    copy_side(("kt", t), kT[:, :, t * P:(t + 1) * P],
                              ps[:, side_bank(("kt", t)), :].rearrange("p (a j) -> p a j", a=PAIRS))

            for j, t in enumerate(range(NT - 1, -1, -1)):
                if t == 5:
                    act.wait_ge(kvc_done, 1)
                if t == 0:
                    hi_to(("q", 3))
                i = MIDX[("v", t)]
                act.wait_ge(main_done, i + 1)
                A(v[:, t, :], ps[:, i % 2, :], ACT.Copy).then_inc(main_free[i % 2], 1)
                if t == 0:
                    hi_to(("g", 1))
                if j:
                    copy_side(("kv", t + 1), kv[:, t + 1, :], ps[:, side_bank(("kv", t + 1)), :])
            copy_side(("kv", 0), kv[:, 0, :], ps[:, side_bank(("kv", 0)), :])

            for j in range(1, 17):
                if j == 7:
                    hi_to(("g", 3))
                if j == 9:
                    hi_to(("u", 1))
                if j == 15:
                    hi_to(("u", 3))
                if j == 16:
                    hi_to(("cs", 1))
                if j <= 8:
                    t = j - 1
                    copy_side(("qt", t), qT[:, :, t * P:(t + 1) * P],
                              ps[:, side_bank(("qt", t)), :].rearrange("p (a j) -> p a j", a=PAIRS))
                if j >= 8 and j - 8 < NT:
                    n = j - 8
                    i = MIDX[("g", n)]
                    if n == 0:
                        act.wait_ge(roped, 2 * NT)
                        act.dma_start(gnb[:], ins["gn_rows"]).then_inc(late_in, 16)
                    if n >= 2:
                        act.wait_ge(r_ready, n - 1)
                    act.wait_ge(main_done, i + 1)
                    A(sg[:, n % 2, :], ps[:, i % 2, :], ACT.Silu).then_inc(main_free[i % 2], 1)
                if 3 <= j <= 10:
                    n = j - 3
                    act.wait_ge(meansq, 10 + n + 1)
                    A(hss[:, :, 2], hss[:, :, 1], ACT.Sqrt).then_inc(root, 1)
                if j == 12:
                    act.wait_ge(masked, 2 * NT)
                    act.dma_start(mcs[:], ins["mcs"]).then_inc(late_in, 16)
                    act.dma_start(sgn[:], ins["sgn"]).then_inc(late_in, 16)

            for g in range(GROUPS):
                i = MIDX[("u", g, 0)]
                act.wait_ge(main_done, i + 1)
                if g:
                    act.wait_ge(ue_ready, g)
                else:
                    act.wait_ge(r_ready, NT)
                A(u_lo[:], ps[:, 0, :], ACT.Copy).then_inc(main_free[0], 1)
                if g == 3:
                    hi_to(("cs", 3))
            hi_to(("gb", 1))
            act.wait_ge(dft_done, 4)
            act.dma_start(wn_raw[:], ins["four_nyq"]).then_inc(wn_in, 16)

            def store_y(m):
                act.wait_ge(y_ready, m + 1)
                act.dma_start(y_scr[m], y[:]).then_inc(y_stored, 16)

            def row_out(a, banks):
                for half in range(2):
                    act.wait_ge(ada_red, 2 * a + half + 1)
                    if a or half:
                        act.wait_ge(row_stored, 16 * (2 * a + half))
                    A(ada_row[:], ps[0:1, banks + half, :], ACT.Copy).then_inc(ada_row_out, 1)
                    act.wait_ge(ada_row_out, 2 * a + half + 1)
                    act.dma_start(mod_scr[a:a + 1, half * 512:(half + 1) * 512], ada_row[:]).then_inc(row_stored, 16)

            def load_ada(j):
                if j:
                    act.wait_ge(ada_acc_done, j)
                act.dma_start(ada_raw[:], ins["w_ada"][(j % 8) * P:(j % 8 + 1) * P, (2 + j // 8) * D:(3 + j // 8) * D]
                              ).then_inc(ada_raw_in, 16)

            for m in range(KT):
                load_ada(4 * m)
                if m + 1 < KT:
                    hi_to(("fr", m + 1))
                act.wait_ge(merge_done, 9 * m + 2)
                if m:
                    act.wait_ge(y_ready, m)
                A(sig_a[:], ps[:, 0:2, :].rearrange("p a b -> p (a b)"), ACT.Sigmoid).then_inc(gates_done, 1)
                load_ada(4 * m + 1)
                hi_to(("ga", m + 2) if m + 2 < KT else ("wo", 2 * (m - 6)))
                load_ada(4 * m + 2)
                if m:
                    store_y(m - 1)
                act.wait_ge(merge_done, 9 * m + 4)
                A(sig_b[:], ps[:, 2:4, :].rearrange("p a b -> p (a b)"), ACT.Sigmoid).then_inc(gates_done, 1)
                load_ada(4 * m + 3)
                if m in (2, 4, 6):
                    row_out(m // 2 - 1, 6)
                hi_to(("gb", m + 2) if m + 2 < KT else ("wo", 2 * (m - 6) + 1))
            for t in range(KT - 1):
                act.wait_ge(y_landed[t], 16)
                A(yT_hi[:, t, :], y_in[:, t, :], ACT.Copy).then_inc(y_hi_done, 1)
            def load_acc(n):
                act.dma_start(acc[:, 2 * n:2 * n + 2, :],
                              ins["x"][2 * n * P:(2 * n + 2) * P, :].rearrange("(t p) d -> p t d", p=P)
                              ).then_inc(acc_in[n], 16)

            act.wait_ge(y7_ready, 1)
            act.dma_start(g1b[:], mod_scr[0:1, :].to_broadcast([P, D])).then_inc(gate1_in, 16)
            act.dma_start(b1b[:], ins["b_ada"][:, 2 * D:3 * D].to_broadcast([P, D])).then_inc(gate1_in, 16)
            act.wait_ge(merge_done, 9 * KT)
            load_acc(0)
            row_out(3, 2)
            hi_to(("wo", 5))
            for n in range(1, 4):
                load_acc(n)
            act.wait_ge(row_stored, 16 * 8)
            act.dma_start(g2b[:], mod_scr[3:4, :].to_broadcast([P, D])).then_inc(gates_in, 16)
            act.dma_start(b2b[:], ins["b_ada"][:, 5 * D:6 * D].to_broadcast([P, D])).then_inc(gates_in, 16)
            with nc.allow_non_contiguous_dma(reason="2048 modulation values, one per row"):
                for a in range(2):
                    act.dma_start(mod2[:, a, :], mod_scr[1 + a, :].rearrange("(c p) -> p c", p=P)).then_inc(gates_in, 16)
            hi_to(("wo", 7))

            def hi_mlp(c, b, dst):
                raw_wait_mlp(act, c, b)
                A(dst, raw[:, (MLP0 + c) % 2, :], ACT.Copy).then_inc(hi_done, 1)

            for c in range(FFB):
                if c < 2:
                    act.wait_ge(*released(("wo", 2 + c)))
                elif c == 2:
                    act.wait_ge(g_ready, 3)
                hi_mlp(c, 0, w1_slot(c)[0])

            def h2_hi_half(u):
                for half in range(2):
                    side_out(act, ("z", u, half))
                A(h2_hi[:, :, u * P:(u + 1) * P], (h2_f, h2_g)[u % 2][:].rearrange("p (c t) -> p c t", c=KT),
                  ACT.Copy).then_inc(hhi_done, 1)

            for t in range(NT + 1):
                if t < NT:
                    act.wait_ge(x2_done, t + 1)
                    act.wait_ge(sumsq, 10 + t)
                    if t == 0:
                        act.wait_ge(gates_done, 2 * KT)
                    A(ps[:, 0:2, :].rearrange("p a b -> p (a b)"), acc[:, t, :], ACT.Square, accum_out=ss[:, t:t + 1]).then_inc(sumsq, 1)
                if t >= 2:
                    h2_hi_half(t - 2)
                if t < NT:
                    act.wait_ge(meansq, 18 + t + 1)
                    A(rt[:, t:t + 1], ms[:, t:t + 1], ACT.Sqrt).then_inc(root, 1)
                    act.wait_ge(rstd_ready, 10 + t + 1)
                    if t >= 2:
                        act.wait_ge(side_done, SIDX[("z", t - 2, 1)] + 1)
                    A((xh, xh_b)[t % 2][:], acc[:, t, :], ACT.Identity, scale=rstd[:, t:t + 1]).then_inc(xhat, 1)

            def relu_square(f, b):
                act.wait_ge(ff_done, b * 8 + (f + 1))
                A(ps[:, f % 2, :], ps[:, f % 2, :], ACT.Relu).then_inc(ff_relu, 1)
                act.wait_ge(ff_relu, b * 8 + (f + 1))
                A(ps[:, f % 2, :], ps[:, f % 2, :], ACT.Square).then_inc(ff_sq, 1)

            def next_w1(c, b):
                act.wait_ge(ff_done, b * 8 + (FFB + c + 1))
                hi_mlp(8 + c, b, w1_slot(c)[0])

            def mlp_block(b, first, last):
                for f in range(first, 8):
                    relu_square(f, b)
                    if 1 <= f <= FFB:
                        if f == 1:
                            act.wait_ge(o_done, b * 16 + 16)
                        act.wait_ge(w2_scaled, b * FFB + f)
                        hi_mlp(FFB + f - 1, b, w2_slot(f - 1)[0])
                    if f > FFB and not last:
                        next_w1(f - FFB - 1, b)
                if not last:
                    next_w1(FFB - 1, b)

            relu_square(0, 0)
            act.wait_ge(o_done, 16)
            act.wait_ge(w2_scaled, 1)
            hi_mlp(FFB, 0, w2_slot(0)[0])
            relu_square(1, 0)
            h2_hi_half(NT - 1)
            mlp_block(0, 2, False)
            with act.Fori(1, BLOCKS - 1) as b:
                mlp_block(b, 0, False)
            mlp_block(BLOCKS - 1, 0, True)
            act.wait_ge(ff_done, 8 * BLOCKS)
            act.dma_start(fgb[:], ins["final_gain"].to_broadcast([P, D])).then_inc(fin_in, 16)
            for t in range(NT):
                act.wait_ge(o_free, 16 * BLOCKS + 2 * t + 2)
                act.wait_ge(sumsq, 18 + t)
                A(junk3[:], acc[:, t, :], ACT.Square, accum_out=ss[:, t:t + 1]).then_inc(sumsq, 1)
                act.wait_ge(meansq, 26 + t + 1)
                A(rt[:, t:t + 1], ms[:, t:t + 1], ACT.Sqrt).then_inc(root, 1)

        @block.vector
        def _(dve):
            do = Steps(dve, dve_step)
            V = nc.vector

            def mean_root(src, dst_m, n, src_r, dst_r, count_in, count_root):
                dve.wait_ge(sumsq, count_in)
                V.tensor_scalar(dst_m, src, 1.0 / n, EPS, ALU.mult, ALU.add).then_inc(meansq, 1)
                dve.wait_ge(root, count_root)
                return V.reciprocal(dst_r, src_r)

            def tokens_norm(s):
                mean_root(ss[:, s:s + 1], ms[:, s:s + 1], D, rt[:, s:s + 1], rstd[:, s:s + 1], s + 1, s + 1
                          ).then_inc(rstd_ready, 1)

            V.memset(ones[:], 1.0).then_inc(mod_ready, 1)
            tokens_norm(0)
            dve.wait_ge(decay_in, 16 * 3)
            do.chain(V.tensor_scalar(lw[:, 0, :], lgt[:], -1.0, None, ALU.mult))
            do.chain(V.tensor_tensor(lw[:, 0, :], lw[:, 0, :], lgt[:], ALU.min), decay_log)
            dve.wait_ge(decay_exp, 1)
            do.chain(V.tensor_scalar(lw[:, 2, :], lw[:, 1, :], 1.0, None, ALU.add), decay_log)
            do(V.reciprocal(lw[:, 5, :], lw[:, 2, :]))
            do.chain(V.tensor_scalar(lw[:, 4, :], lw[:, 2, :], -1.0, None, ALU.add))
            do.chain(V.tensor_tensor(lw[:, 4, :], lw[:, 1, :], lw[:, 4, :], ALU.subtract))
            do.chain(V.tensor_tensor(lw[:, 4, :], lw[:, 4, :], lw[:, 5, :], ALU.mult))
            dve.wait_ge(decay_exp, 2)
            do.chain(V.tensor_tensor(lw[:, 4, :], lw[:, 4, :], lw[:, 3, :], ALU.add))
            do.chain(V.tensor_scalar(lg[:], lgt[:], 0.0, None, ALU.min))
            do.chain(V.tensor_tensor(lg[:], lg[:], lw[:, 4, :], ALU.subtract))
            do.chain(V.tensor_tensor(dec[:], posc[:], lg[:, None, :].to_broadcast([P, 5, 16]), ALU.mult), decay_log)
            dve.wait_ge(decay_exp, 3)
            do.chain(V.tensor_scalar(dec[:, 1:4, :], dec[:, 1:4, :], HD ** -0.5, None, ALU.mult))
            pair_dec = dec[:, 4, :].rearrange("p (d a e) -> p a d e", d=2, e=2)
            do(V.tensor_copy(dec_s[0:64], pair_dec[0:64, :, :, 0]))
            do(V.tensor_copy(dec_s[64:128], pair_dec[64:128, :, :, 1]))
            tokens_norm(1)
            def mask(h):
                dve.wait_ge(decay_exp, 3 + 2 * (h + 1))
                do(V.tensor_tensor(dmask[:, h, :], dtmp[:, h % 2, 0, :], dist[:, 2, :], ALU.mult))
                do.chain(V.tensor_tensor(dtmp[:, h % 2, 2, :], dtmp[:, h % 2, 1, :], dist[:, 3, :], ALU.mult), decay_log)
                do.chain(V.tensor_tensor(dmask[:, h, :], dmask[:, h, :], dtmp[:, h % 2, 2, :], ALU.add))

            for h in range(3):
                mask(h)

            def modulate(a, sh, keys):
                for half, key in enumerate(keys):
                    dve.wait_ge(side_done, SIDX[key] + 1)
                    if half == 0 and h_written[0]:
                        dve.wait_ge(*h_written[0])
                    for q in range(4):
                        c = 4 * half + q
                        ins_ = V.tensor_scalar(h_dst[0][:, c * P:(c + 1) * P],
                                               ps[:, side_bank(key), q * P:(q + 1) * P],
                                               a(c), sh(c), ALU.mult, ALU.add)
                    ins_.then_inc(side_free[SIDX[key] % 2], 1)

            h_dst = [h_f]
            h_written = [None]

            dve.wait_ge(first_in, 16 * 3)
            for q in range(4):
                dve.wait_ge(ada_done, q + 1)
                V.tensor_tensor(mod_rows[:, q * 512:(q + 1) * 512], ps[0:2, 4 + q, :],
                                mod_rows[:, q * 512:(q + 1) * 512], ALU.add).then_inc(rows_done, 1)
            dve.wait_ge(modT_done, 1)
            do.chain(V.tensor_copy(mod[:], ps[:, 0, 0:32].rearrange("p (c r) -> p c r", r=2)))
            do.chain(V.tensor_scalar(a1[:], mod[:, KT:2 * KT, :], 1.0, None, ALU.add))
            V.tensor_tensor(a1[:], a1[:], gain1[:, :, None].to_broadcast([P, KT, 2]), ALU.mult).then_inc(mod_ready, 1)
            dve.wait_ge(mod_ready, 2)

            def rope_tile(src, t, dst, ta, tb, i):
                sv = src.rearrange("p (h e f) -> p h e f", h=HEADS, e=2)
                dv = dst.rearrange("p (h e f) -> p h e f", h=HEADS, e=2)
                av = ta.rearrange("p (h e f) -> p h e f", h=HEADS, e=2)
                bv = tb.rearrange("p (h e f) -> p h e f", h=HEADS, e=2)
                cos = rope[:, t, 0, :][:, None, :].to_broadcast([P, 2 * HEADS, HD // 2])
                sin = rope[:, t, 1, :][:, None, :].to_broadcast([P, 2 * HEADS, HD // 2])
                dve.wait_ge(main_done, i + 1)
                do(V.tensor_tensor(ta.rearrange("p (h f) -> p h f", f=HD // 2),
                                   src.rearrange("p (h f) -> p h f", f=HD // 2), cos, ALU.mult))
                do.chain(V.tensor_tensor(tb.rearrange("p (h f) -> p h f", f=HD // 2),
                                         src.rearrange("p (h f) -> p h f", f=HD // 2), sin, ALU.mult),
                         main_free[i % 2], i // 2 + 1)
                do(V.tensor_tensor(dv[:, :, 0, :], av[:, :, 0, :], bv[:, :, 1, :], ALU.subtract))
                do.chain(V.tensor_tensor(dv[:, :, 1, :], av[:, :, 1, :], bv[:, :, 0, :], ALU.add), roped)

            dve.wait_ge(params_in, 16 * 4)
            for s in range(1, 12):
                if 1 <= s <= 10:
                    n = s - 1
                    r = 1 if n < 2 else 0
                    modulate(lambda c: a1[:, c, r:r + 1], lambda c: mod[:, c, r:r + 1], [("x", n, 0), ("x", n, 1)])
                    h_written[0] = (h_ready, n + 1)
                if 2 <= s < 10:
                    tokens_norm(s)
                for h in {1: (3, 4), 2: (5, 6), 3: (7,)}.get(s, ()):
                    mask(h)
                if s >= 4:
                    t = s - 4
                    i = MIDX[("k", t)]
                    rope_tile(ps[:, i % 2, :], t, kv[:, t, :], t1[:, 0, :], t1[:, 1, :], i)

            def v_decayed(dst, src, r, d):
                g = dec[:, r, 8 * d:8 * d + 8][:, :, None].to_broadcast([P, HEADS, HD])
                return V.tensor_tensor(dst.rearrange("p (h d v) -> p h d v", h=HEADS, d=2)[:, :, d, :],
                                       src.rearrange("p (h v) -> p h v", h=HEADS), g, ALU.mult)

            def roll_state(cur, other, d, t, signal=None):
                g = dec_s[:, :, d][:, :, None].to_broadcast([P, PAIRS, HD])
                kvt = kv[:, t, :].rearrange("p (a d v) -> p a d v", a=PAIRS, d=2)[:, :, d, :]
                do.chain(V.tensor_tensor(other, cur, g, ALU.mult))
                do.chain(V.tensor_tensor(other, other, kvt, ALU.add))
                do.chain(V.tensor_copy(kvt, cur), signal)

            for r in range(2):
                i = MIDX[("v", VTILES[r])]
                dve.wait_ge(main_done, i + 1)
                do(v_decayed(vcat_c[:, r, :], ps[:, i % 2, :], 2 + r, 0), vcat_ready)
                do(v_decayed(vcat_c[:, r, :], ps[:, i % 2, :], 2 + r, 1), main_free[i % 2])
            dve.wait_ge(kvc_done, 1)
            bank7 = ps[:, 7, :].rearrange("p (a d v) -> p a d v", a=PAIRS, d=2)
            cur_b, oth_b = st_b[:, 0], st_b[:, 1]
            do.chain(V.tensor_copy(cur_b, bank7[:, :, 1, :]))
            for j, t in enumerate(range(NT - 1, -1, -1)):
                i = MIDX[("v", t)]
                dve.wait_ge(main_free[i % 2], i // 2 + 1)
                if j >= 2:
                    side_out(dve, ("kv", t + 2))
                for d in range(2):
                    do(v_decayed(vcat[:, j % 2, :], v[:, t, :], 1, d), vcat_ready)
                if j >= 2:
                    roll_state(cur_b, oth_b, 1, t + 2)
                    cur_b, oth_b = oth_b, cur_b
            side_out(dve, ("kv", 1))
            roll_state(cur_b, oth_b, 1, 1)
            cur_b, oth_b = oth_b, cur_b
            side_out(dve, ("kv", 0))
            do.chain(V.tensor_copy(kv[:, 0, :].rearrange("p (a d v) -> p a d v", a=PAIRS, d=2)[:, :, 1, :], cur_b))
            dve.wait_ge(wpm_stored, 16 * 4)
            cur_f, oth_f = st_f[:, 0], st_f[:, 1]
            do.chain(V.tensor_copy(cur_f, bank7[:, :, 0, :]))

            def split_side(n):
                key = ("rt", n)
                dve.wait_ge(side_done, SIDX[key] + 1)
                src = ps[:, side_bank(key), :].rearrange("p (a t) -> p a t", a=PAIRS)
                h_ap, l_ap = rT_hi[:, :, n * P:(n + 1) * P], rT_lo[:, :, n * P:(n + 1) * P]
                do.chain(V.tensor_copy(h_ap, src))
                do(V.tensor_tensor(l_ap, src, h_ap.bitcast(F32), ALU.subtract), side_free[SIDX[key] % 2])

            for j in range(18):
                if 1 <= j <= 8:
                    t = j - 1
                    if t < NT - 1:
                        roll_state(cur_f, oth_f, 0, t, states_ready)
                        cur_f, oth_f = oth_f, cur_f
                    else:
                        do.chain(V.tensor_copy(kv[:, t, :].rearrange("p (a d v) -> p a d v", a=PAIRS, d=2)[:, :, 0, :],
                                               cur_f), states_ready)
                    if t >= 1:
                        dve.wait_ge(side_done, SIDX[("qt", t - 1)] + 1)
                    rope_tile(ps[:, MIDX[("q", t)] % 2, :], t, qa[:], qa[:], qb[:], MIDX[("q", t)])
                if 3 <= j <= 10:
                    n = j - 3
                    dve.wait_ge(inter_done, n + 1)
                    dve.wait_ge(intra_done, n + 1)
                    ov = v[:, n, :].rearrange("p (a e v) -> p a e v", a=PAIRS, e=2)
                    for e in range(2):
                        src = ps[:, 6 + e, :].rearrange("p (a d v) -> p a d v", a=PAIRS, d=2)
                        dq = dec[:, 0, :].rearrange("p (d a e) -> p a d e", d=2, e=2)[:, :, :, e]
                        do.chain(V.tensor_tensor(it[:], src, dq[:, :, :, None].to_broadcast([P, PAIRS, 2, HD]),
                                                 ALU.mult))
                        do.chain(V.tensor_tensor(ov[:, :, e, :], it[:, :, 0, :], it[:, :, 1, :], ALU.add))
                        own = ps[:, 4 + e, :].rearrange("p (a e v) -> p a e v", a=PAIRS, e=2)[:, :, e, :]
                        if e == 0:
                            do.chain(V.tensor_tensor(ov[:, :, e, :], ov[:, :, e, :], own, ALU.add))
                        else:
                            do.chain(V.tensor_tensor(ov[:, :, e, :], ov[:, :, e, :], own, ALU.add), combined)
                    do.chain(V.tensor_tensor(sq[:], v[:, n, :], v[:, n, :], ALU.mult))
                    do.chain(V.tensor_reduce(hss[:, :, 0], sq[:].rearrange("p (h v) -> p h v", h=HEADS), AX.X,
                                             ALU.add))
                    V.tensor_scalar(hss[:, :, 1], hss[:, :, 0], 1.0 / HD, EPS, ALU.mult, ALU.add).then_inc(meansq, 1)
                    dve.wait_ge(root, 10 + n + 1)
                    do.chain(V.reciprocal(hss[:, :, 3], hss[:, :, 2]))
                    do.chain(V.tensor_tensor(v[:, n, :].rearrange("p (h v) -> p h v", h=HEADS),
                                             v[:, n, :].rearrange("p (h v) -> p h v", h=HEADS),
                                             hss[:, :, 3:4].to_broadcast([P, HEADS, HD]), ALU.mult), o_ready)
                if 2 <= j <= 9:
                    n = j - 2
                    dve.wait_ge(scores_done, n + 1)
                    if n:
                        dve.wait_ge(intra_done, n)
                    for e in range(2):
                        src = ps[:, 4 + e, :].rearrange("p (a i) -> p a i", a=PAIRS)
                        av = aT[:].rearrange("p (a e) i -> p a e i", e=2)[:, :, e, :]
                        mv = dmask[:].rearrange("p (a e) i -> p a e i", e=2)[:, :, e, :]
                        V.tensor_tensor(av, src, mv, ALU.mult).then_inc(masked, 1)
                if 9 <= j < 17:
                    n = j - 9
                    if n == 0:
                        dve.wait_ge(late_in, 16)
                    i = MIDX[("g", n)]
                    dve.wait_ge(main_free[i % 2], i // 2 + 1)
                    do.chain(V.tensor_tensor(v[:, n, :], v[:, n, :], gnb[:], ALU.mult))
                    do.chain(V.tensor_tensor(v[:, n, :], v[:, n, :], sg[:, n % 2, :], ALU.mult), r_ready)
                if j >= 11:
                    split_side(j - 11)
            split_side(7)

            dve.wait_ge(late_in, 48)
            for g in range(GROUPS):
                i = MIDX[("u", g, 1)]
                dve.wait_ge(main_free[0], MIDX[("u", g, 0)] // 2 + 1)
                dve.wait_ge(main_done, i + 1)
                up = ps[:, i % 2, :]
                back = up[:, HALF - 1:0:-1]
                do(V.tensor_tensor(u_e[:, g, 1:HALF], u_lo[:, 1:HALF], back, ALU.add))
                do(V.tensor_copy(u_e[:, g, 0:1], u_lo[:, 0:1]))
                do(V.memset(u_o[:, g, 0:1], 0.0))
                do(V.tensor_copy(u_c[:, 0, g:g + 1], up[:, 0:1]))
                do.chain(V.tensor_tensor(u_o[:, g, 1:HALF], u_lo[:, 1:HALF], back, ALU.subtract), main_free[1], i // 2 + 1)
                do.chain(V.tensor_tensor_reduce(fj[:], u_e[:, g, :], sgn[:], 1.0, 0.0, ALU.mult, ALU.add,
                                                u_c[:, 1, g:g + 1]), ue_ready)
            V.scalar_tensor_tensor(u_c[:, 1, :], u_c[:, 0, :], SEQ ** -0.5, u_c[:, 1, :], ALU.mult,
                                   ALU.add).then_inc(uc_ready, 1)

            for nt in range(4):
                for part in range(2):
                    b = 4 + 2 * (nt % 2) + part
                    dve.wait_ge(pq_done, 2 * nt + part + 1)
                    src = ps[:, b, :].rearrange("p (g d) -> p g d", g=GROUPS)
                    if part == 0:
                        do.chain(V.tensor_copy(pn_hi[:, nt, :], src[:, :, 64]))
                        do(V.tensor_tensor(pn_lo[:, nt, :], src[:, :, 64], pn_hi[:, nt, :].bitcast(F32), ALU.subtract))
                    h_ap, l_ap = ((pa_hi, pa_lo), (pb_hi, pb_lo))[part]
                    hv = h_ap[:, nt, :].rearrange("p (g d) -> p g d", g=GROUPS)
                    lv = l_ap[:, nt, :].rearrange("p (g d) -> p g d", g=GROUPS)
                    do.chain(V.tensor_copy(hv, src[:, :, 0:64]))
                    do(V.tensor_tensor(lv, src[:, :, 0:64], hv.bitcast(F32), ALU.subtract), pq_free)
                if nt == 0:
                    dve.wait_ge(cols_done, 1)
                    do.chain(V.tensor_copy(cols[:], ps[:, 3, 0:4].rearrange("p (a r) -> p a r", a=2)))
                    do.chain(V.tensor_copy(cols_n[:], ps[0:GROUPS, 3, 4:8]), cols_free)
                    do.chain(V.tensor_copy(a5_hi[:, :, 0], cols[:, :, 1]))
                    do.chain(V.tensor_copy(a5_hi[:, :, 1], cols[:, :, 1]))
                    do(V.tensor_tensor(a5_lo[:, :, 0], cols[:, :, 1], a5_hi[:, :, 0].bitcast(F32), ALU.subtract))
                    do(V.tensor_tensor(a5_lo[:, :, 1], cols[:, :, 1], a5_hi[:, :, 0].bitcast(F32), ALU.subtract))
                    for q in range(2):
                        do.chain(V.tensor_copy(n5_hi[:, q:q + 1], cols_n[:, 2:3]))
                        do(V.tensor_tensor(n5_lo[:, q:q + 1], cols_n[:, 2:3], n5_hi[:, q:q + 1].bitcast(F32),
                                           ALU.subtract))

            dve.wait_ge(dft_done, 4)
            for p in range(2):
                do.chain(V.scalar_tensor_tensor(ft[:], sgn[:], cols[:, p, 0:1], ps[:, p, :], ALU.mult, ALU.add))
                do.chain(V.tensor_copy(ab_hi[:, p, :], ft[:]))
                do.chain(V.tensor_tensor(ab_lo[:, p, :], ft[:], ab_hi[:, p, :].bitcast(F32), ALU.subtract), ab_ready)
            for p in range(2):
                do.chain(V.tensor_copy(ab_hi[:, 2 + p, :], ps[:, 2 + p, :]))
                do.chain(V.tensor_tensor(ab_lo[:, 2 + p, :], ps[:, 2 + p, :], ab_hi[:, 2 + p, :].bitcast(F32),
                                         ALU.subtract), ab_ready)
            dve.wait_ge(wpm_stored, 16 * KT)
            do.chain(V.scalar_tensor_tensor(ft[0:GROUPS, :], sgn[0:GROUPS, :], cols_n[:, 0:1], ps[0:GROUPS, 4, :],
                                            ALU.mult, ALU.add))
            do.chain(V.tensor_copy(an_hi[:], ft[0:GROUPS, :]))
            do.chain(V.tensor_tensor(an_lo[:], ft[0:GROUPS, :], an_hi[:].bitcast(F32), ALU.subtract), ab_ready)
            dve.wait_ge(wn_in, 16)
            do.chain(V.tensor_copy(wn_hi[:], wn_raw[:]))
            do.chain(V.tensor_tensor(wn_lo[:], wn_raw[:], wn_hi[:].bitcast(F32), ALU.subtract), ab_ready)

            for m in range(KT):
                for a in range(4):
                    jj = 4 * m + a
                    kt = jj % 8
                    dve.wait_ge(ada_raw_in, 16 * (jj + 1))
                    if kt == 0:
                        if jj:
                            dve.wait_ge(ada_red, 2 * (jj // 8))
                        do.chain(V.tensor_scalar(ada_acc[:], ada_raw[:], silu_c[:, 0, 0:1], None, ALU.mult),
                                 ada_acc_done)
                    else:
                        do.chain(V.scalar_tensor_tensor(ada_acc[:], ada_raw[:], silu_c[:, kt, 0:1], ada_acc[:],
                                                        ALU.mult, ALU.add), ada_acc_done)
                dve.wait_ge(merge_done, 9 * m + 7)
                if m:
                    dve.wait_ge(y_stored, 16 * m)
                do.chain(V.tensor_copy(b_sb[:], ps[:, 5, :]))
                do(V.tensor_tensor(y[:, 0:HALF], ps[:, 4, :], b_sb[:], ALU.subtract))
                do(V.tensor_tensor(y[:, SEQ - 1:HALF:-1], ps[:, 4, 1:HALF], b_sb[:, 1:HALF], ALU.add), four_free)
                do.chain(V.tensor_copy(y[:, HALF:HALF + 1], ps[:, 0, 0:1]), col_free)
                dve.wait_ge(gates_done, 2 * m + 2)
                do.chain(V.tensor_tensor(y[:], y[:], sig_a[:], ALU.mult))
                dve.wait_ge(merge_done, 9 * m + 9)
                do.chain(V.tensor_tensor(sig_b[:], sig_b[:], ps[:, 6:8, :].rearrange("p a b -> p (a b)"), ALU.mult),
                         ret_free)
                do.chain(V.tensor_tensor(y[:], y[:], sig_b[:], ALU.add), y_ready)
                if m == KT - 1:
                    do.chain(V.tensor_copy(yT_hi[:, m, :], y[:]))
                    V.tensor_tensor(yT_lo[:, m, :], y[:], yT_hi[:, m, :].bitcast(F32), ALU.subtract).then_inc(y7_ready, 1)
                    dve.wait_ge(y7_ready, 1)

            dve.wait_ge(gate1_in, 16 * 2)
            do.chain(V.tensor_tensor(g1b[:], g1b[:], b1b[:], ALU.add), g_ready)

            def residual(nh, t):
                i = nh * NT + t
                if nh == 0 and t % 2 == 0:
                    dve.wait_ge(acc_in[t // 2], 16)
                dve.wait_ge(o_done, i + 1)
                do.chain(V.tensor_tensor(gated[:], ps[:, 4 + i % 4, :], g1b[:, nh * 512:(nh + 1) * 512], ALU.mult),
                         o_free)
                dst = acc[:, t, nh * 512:(nh + 1) * 512]
                do.chain(V.tensor_tensor(dst, dst, gated[:], ALU.add), x2_done if nh else None)

            do.chain(V.memset(rt[:, 15:16], 0.0), ff_free)
            do.chain(V.memset(rt[:, 15:16], 0.0), ff_free)
            for t in range(NT):
                residual(0, t)
            dve.wait_ge(gates_in, 16 * 4)
            do.chain(V.tensor_tensor(g2b[:], g2b[:], b2b[:], ALU.add), g_ready)
            do.chain(V.tensor_tensor(mod2[:], mod2[:], bmod2[:], ALU.add))
            do.chain(V.tensor_scalar(a2[:], mod2[:, 1, :], 1.0, None, ALU.add))
            do.chain(V.tensor_tensor(a2[:], a2[:], gain2[:], ALU.mult), g_ready)
            def modulate_h2(u):
                h_dst[0] = (h2_f, h2_g)[u % 2]
                h_written[0] = (h_ready, 10 + u - 1) if u >= 2 else None
                modulate(lambda c: a2[:, c:c + 1], lambda c: mod2[:, 0, c:c + 1], [("z", u, 0), ("z", u, 1)])

            for t in range(NT + 1):
                if 1 <= t <= NT:
                    u = t - 1
                    mean_root(ss[:, u:u + 1], ms[:, u:u + 1], D, rt[:, u:u + 1], rstd[:, u:u + 1],
                              10 + u + 1, 18 + u + 1).then_inc(rstd_ready, 1)
                if t < NT:
                    residual(1, t)
                if t >= 2:
                    modulate_h2(t - 2)

            def split_ff(f, b):
                dve.wait_ge(ff_sq, b * 8 + (f + 1))
                dve.wait_ge(o_done, b * 16 + 16)
                half, c = f // FFB, f % FFB
                h_ap, l_ap = ff_hi[:, c, half * 512:(half + 1) * 512], ff_lo[:, c, half * 512:(half + 1) * 512]
                V.tensor_copy(h_ap, ps[:, f % 2, :]).then_inc(ff_hi_done, 1)
                dve.wait_ge(ff_hi_done, b * 8 + (f + 1))
                V.tensor_tensor(l_ap, ps[:, f % 2, :], h_ap.bitcast(F32), ALU.subtract).then_inc(ff_free, 1)

            def add_out(i, b):
                t, nh = i // 2, i % 2
                dst = acc[:, t, nh * 512:(nh + 1) * 512]
                dve.wait_ge(o_done, b * 16 + (16 + i + 1))
                dve.wait_ge(o_free, b * 16 + (i + 1))
                V.tensor_tensor(dst, ps[:, 4 + i % 4, :], dst, ALU.add).then_inc(o_free, 1)

            dve.wait_ge(h_ready, 17)
            split_ff(0, 0)
            split_ff(1, 0)
            modulate_h2(NT - 1)
            dve.wait_ge(h_ready, 18)
            for f in range(2, 8):
                split_ff(f, 0)
            for i in range(16):
                add_out(i, 0)
            with dve.Fori(1, BLOCKS - 1) as b:
                for f in range(8):
                    split_ff(f, b)
                for i in range(16):
                    add_out(i, b)
            b = BLOCKS - 1
            for f in range(8):
                split_ff(f, b)

            def final(t):
                do.chain(mean_root(ss[:, t:t + 1], ms[:, t:t + 1], D, rt[:, t:t + 1], rstd[:, t:t + 1],
                                   18 + t + 1, 26 + t + 1))
                if t == 0:
                    dve.wait_ge(fin_in, 16)
                if t >= 2:
                    dve.wait_ge(out_stored[t % 2], 16 * (t // 2))
                V.scalar_tensor_tensor(o_sb[:, t % 2, :], acc[:, t, :], rstd[:, t:t + 1], fgb[:], ALU.mult,
                                       ALU.mult).then_inc(y_out, 1)

            for t in range(NT):
                add_out(2 * t, b)
                add_out(2 * t + 1, b)
                if t:
                    final(t - 1)
            final(NT - 1)

        @block.tensor
        def _(pe):
            M = nc.tensor.matmul

            def mm3(dst, l_hi, l_lo, r_hi, r_lo, first, last):
                M(dst, lhsT=l_hi, rhs=r_hi, start=first, stop=False)
                M(dst, lhsT=l_hi, rhs=r_lo, start=False, stop=False)
                return M(dst, lhsT=l_lo, rhs=r_hi, start=False, stop=last)

            def chunk(c):
                pe.wait_ge(split, INDEX[c] + 1)
                return slot(c)

            def token_major(last_tile, kind, dst, l_hi, l_lo, middle):
                for kp in range(4):
                    c = (kind, kp)
                    r_hi, r_lo = chunk(c)
                    for e in range(2):
                        kt = 2 * kp + e
                        cols_ = slice(e * 512, (e + 1) * 512)
                        mm = mm3(dst, l_hi[:, kt, :], l_lo[:, kt, :], r_hi[:, cols_], r_lo[:, cols_],
                                 kt == 0, kt == KT - 1)
                    if kp == 3:
                        mm.then_inc(main_done, 1)
                    elif last_tile:
                        mm.then_inc(used, 1)
                    if kp == 1 and middle is not None:
                        middle()

            def channel_major(kind, n, half, dst, done):
                c = (kind, n)
                l_hi, l_lo = chunk(c)
                toks = slice(half * 512, (half + 1) * 512)
                for kt in range(KT):
                    w = slice(kt * P, (kt + 1) * P)
                    mm = mm3(dst, l_hi[:, w], l_lo[:, w], hT_hi[:, kt, toks], hT_lo[:, kt, toks],
                             kt == 0, kt == KT - 1)
                mm.then_inc(done, 1)

            def transposes(key, srcs):
                side_wait(pe, key)
                b = side_bank(key)
                for q, src in enumerate(srcs):
                    tr = nc.tensor.transpose(ps[:, b, q * P:(q + 1) * P], src, ident[:])
                tr.then_inc(side_done, 1)

            def x_transposes(s):
                pe.wait_ge(xhat, s + 1)
                for half in range(2):
                    transposes(("x", s, half), [x_tile(s)[:, (4 * half + q) * P:(4 * half + q + 1) * P]
                                                for q in range(4)])

            def main(key, middle=None):
                i = MIDX[key]
                kind, t = key
                main_wait(pe, i)
                l_hi, l_lo, s = h_tile(t)
                pe.wait_ge(h_ready, s + 1)
                last = {"k": TILES, "v": VTILES, "q": range(NT), "g": range(NT)}[kind][-1]
                token_major(t == last, kind, ps[:, i % 2, :], l_hi, l_lo, middle)

            pe.wait_ge(silu_done, 1)
            for kt in range(KT):
                pe.wait_ge(ada_landed[kt], 16)
                for q in range(4):
                    mm = M(ps[0:2, 4 + q, :], lhsT=silu_c[:, kt, :], rhs=ada_in[:, kt, q * 512:(q + 1) * 512],
                           start=(kt == 0), stop=(kt == KT - 1))
                    if kt == KT - 1:
                        mm.then_inc(ada_done, 1)
                if kt == KT - 2:
                    pe.wait_ge(first_in, 16 * 3)
                    x_transposes(0)
            pe.wait_ge(rows_done, 4)
            for c in range(2 * KT):
                tr = nc.tensor.transpose(ps[:, 0, 2 * c:2 * c + 2], mod_rows[:, c * P:(c + 1) * P], ident[0:2, 0:2])
            tr.then_inc(modT_done, 1)

            def k_transposes(t):
                pe.wait_ge(roped, t + 1)
                transposes(("kt", t), [kv[:, t, q * P:(q + 1) * P] for q in range(4)])

            x_transposes(1)
            pe.wait_ge(mod_ready, 2)
            for s in range(10):
                main(("k", TILES[s]))
                if s >= 3:
                    k_transposes(s - 3)
                if s + 2 < 10:
                    x_transposes(s + 2)

            def kv_product(t):
                key = ("kv", t)
                side_wait(pe, key)
                pe.wait_ge(vcat_ready, 2 + 2 * (NT - t))
                for h in range(HEADS):
                    lo_p, a = HD * (h % 2), h // 2
                    mm = M(ps[lo_p:lo_p + HD, side_bank(key), a * P:(a + 1) * P],
                           lhsT=kv[:, t, h * HD:(h + 1) * HD],
                           rhs=vcat[:, (NT - 1 - t) % 2, h * P:(h + 1) * P], start=True, stop=True)
                mm.then_inc(side_done, 1)

            for j, t in enumerate(VTILES):
                main(("v", t))
                if j == 0:
                    k_transposes(7)
                if j == 2:
                    pe.wait_ge(vcat_ready, 2)
                    for r in range(2):
                        i = MIDX[("v", VTILES[r])]
                        pe.wait_ge(main_free[i % 2], i // 2 + 1)
                        i = MIDX[("k", TILES[r])]
                        pe.wait_ge(main_free[i % 2], i // 2 + 1)
                    for h in range(HEADS):
                        lo_p, a = HD * (h % 2), h // 2
                        for r in range(2):
                            mm = M(ps[lo_p:lo_p + HD, 7, a * P:(a + 1) * P],
                                   lhsT=k_c[:, r, h * HD:(h + 1) * HD],
                                   rhs=vcat_c[:, r, h * P:(h + 1) * P], start=(r == 0), stop=(r == 1))
                    mm.then_inc(kvc_done, 1)
                if j >= 3:
                    kv_product(VTILES[j - 1])

            def head_rows(x, h, cols_):
                return x[HD * (h % 2):HD * (h % 2) + HD, h // 2, cols_]

            def scores(n):
                toks = slice(n * P, (n + 1) * P)
                if n:
                    pe.wait_ge(combined, n)
                side_out(pe, ("qt", n))
                side_out(pe, ("kt", n))
                for h in range(HEADS):
                    mm = M(ps[:, 4 + h % 2, (h // 2) * P:(h // 2 + 1) * P],
                           lhsT=head_rows(kT, h, toks), rhs=head_rows(qT, h, toks), start=True, stop=True)
                mm.then_inc(scores_done, 1)

            def inter(n):
                if n:
                    pe.wait_ge(combined, n)
                side_out(pe, ("qt", n))
                pe.wait_ge(states_ready, n + 1)
                toks = slice(n * P, (n + 1) * P)
                for h in range(HEADS):
                    a = h // 2
                    mm = M(ps[:, 6 + h % 2, a * P:(a + 1) * P], lhsT=head_rows(qT, h, toks),
                           rhs=kv[HD * (h % 2):HD * (h % 2) + HD, n, a * P:(a + 1) * P], start=True, stop=True)
                mm.then_inc(inter_done, 1)

            def intra(n):
                pe.wait_ge(masked, 2 * (n + 1))
                for h in range(HEADS):
                    a = h // 2
                    mm = M(ps[:, 4 + h % 2, a * P:(a + 1) * P], lhsT=aT[:, h, :],
                           rhs=v[:, n, a * P:(a + 1) * P], start=True, stop=True)
                mm.then_inc(intra_done, 1)

            for j in range(18):
                middle = (lambda n=j - 3: intra(n)) if 3 <= j <= 10 else None
                if j < 2 * NT:
                    main(("q", j) if j < NT else ("g", j - NT), middle)
                elif j == 16:
                    main_wait(pe, MIDX[("u", 0, 0)])
                    channel_major("u", 0, 0, ps[:, 0, :], main_done)
                if j == 0:
                    kv_product(0)
                if 1 <= j <= 8:
                    t = j - 1
                    pe.wait_ge(roped, NT + t + 1)
                    transposes(("qt", t), [qa[:, q * P:(q + 1) * P] for q in range(4)])
                if 2 <= j <= 9:
                    inter(j - 2)
                    scores(j - 2)
                if 10 <= j <= 17:
                    n = j - 10
                    pe.wait_ge(r_ready, n + 1)
                    transposes(("rt", n), [v[:, n, q * P:(q + 1) * P] for q in range(4)])

            for g in range(GROUPS):
                for half in range(2):
                    if g + half:
                        main_wait(pe, MIDX[("u", g, half)])
                        channel_major("u", g, half, ps[:, half, :], main_done)

            pe.wait_ge(late_in, 48)
            for nt in range(4):
                for part in range(2):
                    if nt >= 2:
                        pe.wait_ge(pq_free, 2 * (nt - 2) + part + 1)
                    src = (u_e, u_o)[part]
                    for g in range(GROUPS):
                        if nt == 0 and part == 0:
                            pe.wait_ge(ue_ready, g + 1)
                        mm = M(ps[:, 4 + 2 * (nt % 2) + part, g * P:(g + 1) * P],
                               lhsT=src[:, g, nt * P:(nt + 1) * P], rhs=mcs[:, part, :], start=True, stop=True)
                    mm.then_inc(pq_done, 1)
                if nt == 0:
                    pe.wait_ge(uc_ready, 1)
                    side_out(pe, ("rt", 6))
                    side_out(pe, ("rt", 7))
                    for g in range(GROUPS):
                        M(ps[HD * (g % 2):HD * (g % 2) + HD, 3, 2 * (g // 2):2 * (g // 2) + 2],
                          lhsT=mcs[:, 0, 0:64], rhs=u_c[:, :, g], start=True, stop=True)
                    for r in range(2):
                        mm = M(ps[0:GROUPS, 3, 4 + 2 * r:6 + 2 * r], lhsT=u_c[:, r, :], rhs=mcs[:, 0, 64:66],
                               start=True, stop=True)
                    mm.then_inc(cols_done, 1)

            pe.wait_ge(main_free[1], MIDX[("u", 3, 1)] // 2 + 1)
            pe.wait_ge(main_free[0], MIDX[("u", 3, 0)] // 2 + 1)
            pe.wait_ge(cols_free, 1)
            for nt in range(4):
                pe.wait_ge(pq_free, 2 * nt + 2)
                r_hi, r_lo = chunk(("cs", nt))
                first, last = nt == 0, nt == 3
                for part in range(2):
                    l_hi, l_lo = ((pa_hi, pa_lo), (pb_hi, pb_lo))[part]
                    cs = slice(part * 512, (part + 1) * 512)
                    for p in range(2):
                        w = slice(p * P, (p + 1) * P)
                        mm3(ps[:, 2 * part + p, :], l_hi[:, nt, w], l_lo[:, nt, w], r_hi[:, cs], r_lo[:, cs],
                            first, last)
                if nt == 0:
                    pe.wait_ge(pq_free, 5)
                mm3(ps[0:GROUPS, 4, :], pn_hi[:, nt, :], pn_lo[:, nt, :], r_hi[:, 0:512], r_lo[:, 0:512],
                    first, last).then_inc(dft_done, 1)

            def reduce_row(a, bank):
                pe.wait_ge(ada_acc_done, 8 * (a + 1))
                for half in range(2):
                    M(ps[0:1, bank + half, :], lhsT=ones[:], rhs=ada_acc[:, half * 512:(half + 1) * 512],
                      start=True, stop=True).then_inc(ada_red, 1)

            for m in range(KT):
                for half in range(2):
                    if m:
                        if half == 0:
                            pe.wait_ge(col_free, m)
                    else:
                        pe.wait_ge(ab_ready, 1 + half)
                    channel_major("ga", m, half, ps[:, half, :], merge_done)
                if m in (2, 4, 6):
                    pe.wait_ge(ret_free, m)
                    reduce_row(m // 2 - 1, 6)
                for half in range(2):
                    if m:
                        pe.wait_ge(gates_done, 2 * m)
                    else:
                        pe.wait_ge(ab_ready, 3 + half)
                    channel_major("gb", m, half, ps[:, 2 + half, :], merge_done)
                w_hi, w_lo = chunk(("fr", m))
                ms_ = slice(m * P, (m + 1) * P)
                if m == 0:
                    pe.wait_ge(ab_ready, 6)
                else:
                    pe.wait_ge(four_free, m)
                for p in range(2):
                    w = slice(p * P, (p + 1) * P)
                    mm3(ps[:, 4, :], w_hi[:, w], w_lo[:, w], ab_hi[:, p, :], ab_lo[:, p, :], p == 0, False)
                mm3(ps[:, 4, :], wn_hi[:, ms_], wn_lo[:, ms_], an_hi[:], an_lo[:], False, True).then_inc(merge_done, 1)
                for p in range(2):
                    w = slice((2 + p) * P, (3 + p) * P)
                    mm = mm3(ps[:, 5, :], w_hi[:, w], w_lo[:, w], ab_hi[:, 2 + p, :], ab_lo[:, 2 + p, :],
                             p == 0, p == 1)
                mm.then_inc(merge_done, 1)
                pe.wait_ge(gates_done, 2 * m + 1)
                for p in range(2):
                    w = slice(p * P, (p + 1) * P)
                    mm3(ps[:, 0, 0:2], w_hi[:, w], w_lo[:, w], a5_hi[:, p, :], a5_lo[:, p, :], p == 0, False)
                mm3(ps[:, 0, 0:2], wn_hi[:, ms_], wn_lo[:, ms_], n5_hi[:], n5_lo[:], False, True
                    ).then_inc(merge_done, 1)
                if m % 2:
                    pe.wait_ge(ret_free, m)
                for half in range(2):
                    if m in (2, 4, 6):
                        pe.wait_ge(ada_row_out, m - 1 + half)
                    toks = slice(half * 512, (half + 1) * 512)
                    for kt in range(4):
                        w = slice((4 + kt) * P, (5 + kt) * P)
                        mm = mm3(ps[:, 6 + half, :], w_hi[:, w], w_lo[:, w], rT_hi[:, kt, toks],
                                 rT_lo[:, kt, toks], kt == 0, kt == 3)
                    mm.then_inc(merge_done, 1)
            pe.wait_ge(gates_done, 2 * KT)
            reduce_row(3, 2)

            def z_transposes(t):
                pe.wait_ge(xhat, 10 + t + 1)
                for half in range(2):
                    transposes(("z", t, half), [(xh, xh_b)[t % 2][:, (4 * half + q) * P:(4 * half + q + 1) * P]
                                                for q in range(4)])

            pe.wait_ge(ret_free, KT)
            def out_step(nh, t, kp):
                i = nh * NT + t
                toks = slice(t * P, (t + 1) * P)
                r_hi, r_lo = chunk(("wo", 4 * nh + kp))
                if i == 0:
                    pe.wait_ge(y_split, min(2 * kp + 2, KT - 1))
                for e in range(2):
                    kt = 2 * kp + e
                    if i == 0 and kt == KT - 1:
                        pe.wait_ge(y7_ready, 1)
                    cs = slice(e * 512, (e + 1) * 512)
                    mm = mm3(ps[:, 4 + i % 4, :], yT_hi[:, kt, toks], yT_lo[:, kt, toks], r_hi[:, cs],
                             r_lo[:, cs], kt == 0, kt == KT - 1)
                if kp == 3:
                    mm.then_inc(o_done, 1)
                elif t == NT - 1:
                    mm.then_inc(used, 1)

            for kp in range(4):
                for t in range(4):
                    out_step(0, t, kp)
            for i in range(4, 2 * NT):
                nh, t = i // NT, i % NT
                pe.wait_ge(o_free, i - 3)
                for kp in range(4):
                    out_step(nh, t, kp)
                if nh and t >= 2:
                    z_transposes(t - 2)
            z_transposes(NT - 2)

            def up(f, b):
                half, c = f // FFB, f % FFB
                pe.wait_ge(ff_free, b * 8 + (f + 1))
                pe.wait_ge(split, b * 8 + (MLP0 + c + 1))
                l_hi, l_lo = w1_slot(c)
                toks = slice(half * 512, (half + 1) * 512)
                for kt in range(KT):
                    w = slice(kt * P, (kt + 1) * P)
                    mm = mm3(ps[:, f % 2, :], l_hi[:, w], l_lo[:, w], h2_hi[:, kt, toks], h2_lo[:, kt, toks],
                             kt == 0, kt == KT - 1)
                mm.then_inc(ff_done, 1)

            def down(i, b):
                t, nh = i // 2, i % 2
                pe.wait_ge(o_free, b * 16 + (16 + i - 3))
                for c in range(FFB):
                    if i == 0:
                        pe.wait_ge(split, b * 8 + (MLP0 + FFB + c + 1))
                        pe.wait_ge(ff_free, b * 8 + (2 + c + 1))
                    if i == 8:
                        pe.wait_ge(ff_free, b * 8 + (2 + FFB + c + 1))
                    r_hi, r_lo = w2_slot(c)
                    toks, cs = slice(t * P, (t + 1) * P), slice(nh * 512, (nh + 1) * 512)
                    mm = mm3(ps[:, 4 + i % 4, :], ff_hi[:, c, toks], ff_lo[:, c, toks], r_hi[:, cs], r_lo[:, cs],
                             c == 0, c == FFB - 1)
                mm.then_inc(o_done, 1)

            def downs(b):
                for i in range(16):
                    down(i, b)

            pe.wait_ge(sumsq, 18)
            for f in range(8):
                if f % FFB == 0:
                    pe.wait_ge(h_ready, 14 + f)
                up(f, 0)
                if f == 1:
                    z_transposes(NT - 1)
            downs(0)
            with pe.Fori(1, BLOCKS) as b:
                for f in range(8):
                    up(f, b)
                downs(b)


def constants():
    i = np.arange(P, dtype=np.float64)
    posc = np.zeros((P, 5, 16))
    posc[:, 0, :8], posc[:, 0, 8:] = (i + 1)[:, None], (P - i)[:, None]
    posc[:, 1, :8], posc[:, 1, 8:] = (P - 1 - i)[:, None], i[:, None]
    for r in range(2):
        posc[:, 2 + r, :8], posc[:, 2 + r, 8:] = (CTX - 1 - r * P - i)[:, None], (r * P + i)[:, None]
    posc[:, 4, :] = P
    diff = i[None, :] - i[:, None]
    dist = np.stack([np.maximum(diff, 0), np.maximum(-diff, 0), (diff >= 0) * HD ** -0.5, (diff <= 0) * HD ** -0.5], 1)
    nf = HD // 4
    inv = np.float32(10000.0) ** (-np.arange(nf, dtype=np.float32) / np.float32(nf))
    tok = np.arange(SEQ)
    ang = np.concatenate([(tok // 64).astype(np.float32)[:, None] * inv, (tok % 64).astype(np.float32)[:, None] * inv],
                         -1).astype(np.float64)
    rope = np.stack([np.cos(ang), np.sin(ang)], 1).reshape(NT, P, 2, HD // 2).transpose(1, 0, 2, 3)
    c = np.arange(P)[:, None]
    mcs = np.zeros((P, 2, P))
    mcs[:, 0, :65] = np.cos(2 * np.pi * ((c * np.arange(65)) % P) / P) * P ** -0.5
    mcs[:, 1, :64] = np.sin(2 * np.pi * ((c * np.arange(64)) % P) / P) * P ** -0.5
    n = np.arange(HALF)
    ph = 2 * np.pi * ((n[:, None] * n[None, :]) % SEQ) / SEQ
    dft = np.concatenate([np.cos(ph), np.sin(ph)], 1).reshape(4, P, CW) * SEQ ** -0.5
    sgn = np.broadcast_to((1 - 2 * (n % 2)) * SEQ ** -0.5, (P, HALF))
    coef = np.ones((P, 4))
    coef[0, :2] = coef[64, :2] = 0
    coef[:, 2:] = -1
    out = {"posc": posc, "dist": dist, "rope": rope, "mcs": mcs, "dft": dft, "sgn": sgn, "coef": coef,
           "ident": np.eye(P)}
    return {k: np.ascontiguousarray(a, dtype=np.float32) for k, a in out.items()}


def layouts(a):
    w_in, w_out = a["w_in"][0], a["w_out"][0]

    def token_major(w, col):
        return w[:, col:col + 512].reshape(4, 2, P, 512).transpose(0, 2, 1, 3).reshape(4, P, CW)

    def channel_major(w, col):
        return w[:, col:col + P].reshape(KT, P, P).transpose(1, 0, 2).reshape(P, CW)

    part = {"k": 2 * RW, "v": 3 * RW, "q": RW, "g": 4 * RW, "u": 0, "ga": 5 * RW, "gb": 5 * RW + D}
    chunks = []
    for kind, i in STREAM:
        if kind in ("k", "v", "q", "g"):
            chunks.append(token_major(w_in, part[kind])[i])
        elif kind in ("u", "ga", "gb"):
            chunks.append(channel_major(w_in, part[kind] + i * P))
        elif kind == "wo":
            chunks.append(token_major(w_out, 512 * (i // 4))[i % 4])
    w4 = a["four_w_out"][0]
    rows, partners = [], []
    for tile in range(4):
        for g in (2 * (tile % 2), 2 * (tile % 2) + 1):
            for d in range(64):
                rows.append(g * P + d)
                partners.append(g * P + (P - d) % P)

    def by_tile(idx):
        return w4[np.array(idx)].reshape(4, P, KT, P).transpose(2, 1, 0, 3)

    col = lambda v: np.ascontiguousarray(v.reshape(-1, P).T)
    b_ada = a["b_ada"]
    return {
        "x": a["x"][0], "ctx": a["ctx"][0],
        "cc": np.stack([a["c"][0], a["c_ctx"]], -1).reshape(KT, P, 2).transpose(1, 0, 2),
        "w_ada": a["w_ada"][0], "b_ada": b_ada,
        "b_rows": np.concatenate([b_ada[:, :2 * D], b_ada[:, :2 * D]], 0),
        "bmod2": b_ada[0, 3 * D:5 * D].reshape(2, KT, P).transpose(2, 0, 1),
        "gain1": col(a["norm1_gain"][0]), "gain2": col(a["norm2_gain"][0]),
        "logits": np.broadcast_to(a["ret_decay_logit"][0].reshape(1, 16), (P, 16)),
        "gn_rows": np.broadcast_to(a["ret_gn_gain"], (P, RW)),
        "final_gain": a["final_gain"][None, :],
        "w_stream": np.stack(chunks),
        "four_stream": np.stack([by_tile(rows), by_tile(partners)], 2).reshape(KT, P, 2, 512),
        "four_nyq": w4[64::P],
        "ret_stream": a["ret_w_out"][0].reshape(4, P, KT, P).transpose(2, 1, 0, 3).reshape(KT, P, 512),
        "w1_stream": a["w_mlp1"][0].reshape(KT, P, DFF // P, P).transpose(2, 1, 0, 3).reshape(DFF // P, P, CW),
        "w2_stream": a["w_mlp2"][0].reshape(DFF // P, P, D),
    }


def build(nc, shapes):
    ins = {k: nc.dram_tensor(f"in_{k}", s, F32, kind="ExternalInput").ap() for k, s in shapes.items()}
    out = nc.dram_tensor("out", (SEQ, D), F32, kind="ExternalOutput").ap()
    program(nc, ins, out)


def kernel(**inputs):
    import concourse.bacc as bacc
    from concourse.bass_utils import run_bass_kernel_spmd

    arrays = layouts({k: np.asarray(v) for k, v in inputs.items()})
    arrays.update(constants())
    arrays = {k: np.ascontiguousarray(v) for k, v in arrays.items()}
    nc = bacc.Bacc("TRN2", target_bir_lowering=False, num_devices=1)
    build(nc, {k: v.shape for k, v in arrays.items()})
    r = run_bass_kernel_spmd(nc, [{f"in_{k}": v for k, v in arrays.items()}], core_ids=[0])
    return r.results[0]["out"].reshape(1, SEQ, D)
```
